# Optimizing a Trainium2 kernel written in Bass

```python
import jax
import jax.numpy as jnp
from jax import lax
import numpy as np

D_MODEL = 1024
BATCH = 1
SEQ = 256
DEPTH = 2

MEM_LEN = 256
HEAD_DIM = 64
BRANCH_WIDTH = D_MODEL // 2
N_BRANCH = 3
RW_HEADS = BRANCH_WIDTH // HEAD_DIM
RW_WIDTH = RW_HEADS * HEAD_DIM
RW_DECAY_LORA = 64
RW_AAA_LORA = 64
RW_MV_LORA = 32
RW_GATE_LORA = 128
RW_LNX_EPS = 1e-5 * HEAD_DIM
RW_COLS = 3 * RW_WIDTH + RW_DECAY_LORA + RW_AAA_LORA + RW_GATE_LORA
RW_SPLITS = [RW_WIDTH, 2 * RW_WIDTH, 3 * RW_WIDTH, 3 * RW_WIDTH + RW_DECAY_LORA, 3 * RW_WIDTH + RW_DECAY_LORA + RW_AAA_LORA]
MB_HEADS = BRANCH_WIDTH // HEAD_DIM
MB_WIDTH = MB_HEADS * HEAD_DIM
MB_BLOCK = 256
MB_TOPK = 3
MB_QCHUNK = 32
MB_COLS = 3 * MB_WIDTH
SW_Q_HEADS = BRANCH_WIDTH // HEAD_DIM
SW_KV_HEADS = SW_Q_HEADS // 4
SW_WIDTH = SW_Q_HEADS * HEAD_DIM
SW_KV_WIDTH = SW_KV_HEADS * HEAD_DIM
SW_WINDOW = 128
SW_COLS = SW_WIDTH + 2 * SW_KV_WIDTH
GATE_COLS = N_BRANCH * D_MODEL
IN_COLS = RW_COLS + MB_COLS + SW_COLS + GATE_COLS
XA_HEADS = 4
XA_HEAD_DIM = 128
XA_WIDTH = XA_HEADS * XA_HEAD_DIM
D_FF = 4 * D_MODEL
ROPE_THETA = 10000.0
NORM_EPS = 1e-6
MASK_VALUE = -1e30

kernel_name = 'hybrid_rwkv7_moba_swa_gated_block'

def rms_norm(x, g):
    xf = x.astype(jnp.float32)
    y = xf * lax.rsqrt(jnp.mean(jnp.square(xf), axis=-1, keepdims=True) + NORM_EPS)
    return (y * g.astype(jnp.float32)).astype(x.dtype)

def rope_tables(positions):
    inv_freq = 1.0 / (ROPE_THETA ** (jnp.arange(0, HEAD_DIM, 2, dtype=jnp.float32) / HEAD_DIM))
    ang = positions.astype(jnp.float32)[..., None] * inv_freq
    return jnp.cos(ang), jnp.sin(ang)

def apply_rope(t, cos, sin):
    tf = t.astype(jnp.float32)
    t1, t2 = jnp.split(tf, 2, axis=-1)
    c = cos[:, :, None, :]
    s = sin[:, :, None, :]
    return jnp.concatenate([t1 * c - t2 * s, t2 * c + t1 * s], axis=-1).astype(t.dtype)

def token_shift_lerp(u, mu):
    prev = jnp.pad(u, ((0, 0), (1, 0), (0, 0)))[:, :-1]
    return u + mu * (prev - u)

def rwkv7_scan(r, w, k, v, kk, a):
    B, S, H, N = r.shape

    def step(state, inp):
        r_t, w_t, k_t, v_t, kk_t, a_t = inp
        sa = jnp.einsum('bhvk,bhk->bhv', state, -kk_t)
        state = (state * w_t[:, :, None, :]
                 + sa[..., :, None] * (kk_t * a_t)[:, :, None, :]
                 + v_t[..., :, None] * k_t[:, :, None, :])
        return state, jnp.einsum('bhvk,bhk->bhv', state, r_t)

    xs = tuple(jnp.moveaxis(t, 1, 0) for t in (r, w, k, v, kk, a))
    _, out = lax.scan(step, jnp.zeros((B, H, N, N), jnp.float32), xs)
    return jnp.moveaxis(out, 0, 1)

def rwkv7_branch(u, mu, w0, w_up, a0, a_up, g_up, k_k, k_a, r_k, lnx_w, lnx_b, v_first, v_gate):
    B, S, _ = u.shape
    H, N = RW_HEADS, HEAD_DIM
    f32 = jnp.float32
    u = token_shift_lerp(u, mu)
    r, k, v, xw, xa, xg = jnp.split(u, RW_SPLITS, axis=-1)
    w_log = -jax.nn.softplus(-(w0 + jnp.tanh(xw) @ w_up).astype(f32)) - 0.5
    decay = jnp.exp(-jnp.exp(w_log))
    a = jax.nn.sigmoid((a0 + xa @ a_up).astype(f32))
    g = jax.nn.sigmoid(xg) @ g_up
    if v_gate is not None:
        v = v + (v_first - v) * v_gate
    kk = (k * k_k).astype(f32).reshape(B, S, H, N)
    kk = kk / jnp.maximum(jnp.sqrt(jnp.sum(kk * kk, axis=-1, keepdims=True)), 1e-12)
    k_eff = k.astype(f32) * (1.0 + (a - 1.0) * k_a)

    def heads(t):
        return t.astype(f32).reshape(B, S, H, N)

    rh, kh, vh, wh, ah = heads(r), heads(k_eff), heads(v), heads(decay), heads(a)
    out = rwkv7_scan(rh, wh, kh, vh, kk, ah)
    mean = jnp.mean(out, axis=-1, keepdims=True)
    var = jnp.mean(jnp.square(out - mean), axis=-1, keepdims=True)
    out = ((out - mean) * lax.rsqrt(var + RW_LNX_EPS)).reshape(B, S, RW_WIDTH) * lnx_w + lnx_b
    bonus = (jnp.sum(rh * kh * r_k, axis=-1, keepdims=True) * vh).reshape(B, S, RW_WIDTH)
    o = ((out + bonus) * g.astype(f32)).astype(u.dtype)
    return o, v

def moba_attention(q, k, v):
    B, S, H, hd = q.shape
    nb = -(-S // MB_BLOCK)
    s_pad = nb * MB_BLOCK
    pad = ((0, 0), (0, 0), (0, s_pad - S), (0, 0))
    qh = (q * hd ** -0.5).transpose(0, 2, 1, 3)
    kp = jnp.pad(k.transpose(0, 2, 1, 3), pad)
    vp = jnp.pad(v.transpose(0, 2, 1, 3), pad)
    kb = kp.reshape(B, H, nb, MB_BLOCK, hd)
    vb = vp.reshape(B, H, nb, MB_BLOCK, hd)
    k_mean = jnp.mean(kb.astype(jnp.float32), axis=3).astype(k.dtype)
    top_k = min(MB_TOPK, max(nb - 1, 1))
    b_idx = jnp.arange(B)[:, None, None, None]
    h_idx = jnp.arange(H)[None, :, None, None]
    blk_ids = jnp.arange(nb)
    own_offsets = jnp.arange(MB_BLOCK)

    def chunk(c):
        q0 = c * MB_QCHUNK
        own = q0 // MB_BLOCK
        qc = lax.dynamic_slice_in_dim(qh, q0, MB_QCHUNK, axis=2)
        q_pos = q0 + jnp.arange(MB_QCHUNK)
        gate = jnp.einsum('bhqd,bhnd->bhqn', qc, k_mean).astype(jnp.float32)
        gate = jnp.where(blk_ids < own, gate, MASK_VALUE)
        _, idx = lax.top_k(gate, top_k)
        sel_ok = idx < own
        k_sel = kb[b_idx, h_idx, idx]
        v_sel = vb[b_idx, h_idx, idx]
        s_sel = jnp.einsum('bhqd,bhqjkd->bhqjk', qc, k_sel).astype(jnp.float32)
        s_sel = jnp.where(sel_ok[..., None], s_sel, MASK_VALUE).reshape(B, H, MB_QCHUNK, top_k * MB_BLOCK)
        k_own = lax.dynamic_slice_in_dim(kp, own * MB_BLOCK, MB_BLOCK, axis=2)
        v_own = lax.dynamic_slice_in_dim(vp, own * MB_BLOCK, MB_BLOCK, axis=2)
        k_pos = own * MB_BLOCK + own_offsets
        s_own = jnp.einsum('bhqd,bhkd->bhqk', qc, k_own).astype(jnp.float32)
        s_own = jnp.where(k_pos[None, :] <= q_pos[:, None], s_own, MASK_VALUE)
        p = jax.nn.softmax(jnp.concatenate([s_sel, s_own], axis=-1), axis=-1).astype(v.dtype)
        p_sel = p[..., :top_k * MB_BLOCK].reshape(B, H, MB_QCHUNK, top_k, MB_BLOCK)
        p_own = p[..., top_k * MB_BLOCK:]
        return (jnp.einsum('bhqjk,bhqjkd->bhqd', p_sel, v_sel)
                + jnp.einsum('bhqk,bhkd->bhqd', p_own, v_own))

    out = lax.map(chunk, jnp.arange(S // MB_QCHUNK))
    return out.transpose(1, 0, 3, 2, 4).reshape(B, S, H * hd)

def swa_sink_attention(q, k, v, sinks):
    B, S, HQ, hd = q.shape
    HKV = k.shape[2]
    G = HQ // HKV
    W = SW_WINDOW
    nblk = S // W
    qb = (q * hd ** -0.5).reshape(B, nblk, W, HKV, G, hd)

    def with_prev(t):
        tb = t.reshape(B, nblk, W, HKV, hd)
        prev = jnp.pad(tb, ((0, 0), (1, 0), (0, 0), (0, 0), (0, 0)))[:, :-1]
        return jnp.concatenate([prev, tb], axis=2)

    kk = with_prev(k)
    vv = with_prev(v)
    s = jnp.einsum('bnqhgd,bnkhd->bnhgqk', qb, kk).astype(jnp.float32)
    q_rel = jnp.arange(W)[:, None] + W
    k_rel = jnp.arange(2 * W)[None, :]
    dist = q_rel - k_rel
    band = (dist >= 0) & (dist < W)
    has_prev = (jnp.arange(nblk) > 0)[:, None, None]
    mask = band[None] & (has_prev | (k_rel >= W)[None])
    s = jnp.where(mask[None, :, None, None], s, MASK_VALUE)
    sink = jnp.broadcast_to(sinks.astype(jnp.float32).reshape(HKV, G)[None, None, :, :, None, None],
                            s.shape[:-1] + (1,))
    p = jax.nn.softmax(jnp.concatenate([s, sink], axis=-1), axis=-1)[..., :-1].astype(v.dtype)
    o = jnp.einsum('bnhgqk,bnkhd->bnqhgd', p, vv)
    return o.reshape(B, S, HQ * hd)

def memory_cross_attention(h, mem_n, wq, wk, wv, wo):
    B, S, _ = h.shape
    M = mem_n.shape[1]
    q = (h @ wq).reshape(B, S, XA_HEADS, XA_HEAD_DIM) * XA_HEAD_DIM ** -0.5
    k = (mem_n @ wk).reshape(B, M, XA_HEADS, XA_HEAD_DIM)
    v = (mem_n @ wv).reshape(B, M, XA_HEADS, XA_HEAD_DIM)
    s = jnp.einsum('bshd,bmhd->bhsm', q, k).astype(jnp.float32)
    p = jax.nn.softmax(s, axis=-1).astype(v.dtype)
    o = jnp.einsum('bhsm,bmhd->bshd', p, v).reshape(B, S, XA_WIDTH)
    return o @ wo

def squared_relu_mlp(h, w_up, w_down):
    return jnp.square(jax.nn.relu(h @ w_up)) @ w_down

def setup_inputs(seed: int = 0) -> dict:
    key = jax.random.key(seed)
    keys = iter(jax.random.split(key, 48))
    L = DEPTH
    D = D_MODEL
    f32 = jnp.float32

    def dense(shape, fan_in, scale=1.0):
        return jax.random.normal(next(keys), shape, f32) * (scale * fan_in ** -0.5)

    def gain(shape):
        return 1.0 + 0.02 * jax.random.normal(next(keys), shape, f32)

    def noise(shape, scale):
        return scale * jax.random.normal(next(keys), shape, f32)

    def unif(shape, lo, hi):
        return jax.random.uniform(next(keys), shape, f32, lo, hi)

    x = jax.random.normal(next(keys), (BATCH, SEQ, D), f32)
    mem = jax.random.normal(next(keys), (BATCH, MEM_LEN, D), f32)
    offset = jax.random.randint(next(keys), (BATCH, 1), 0, 4096, jnp.int32)
    positions = (jnp.arange(SEQ, dtype=jnp.int32)[None, :] + offset).astype(jnp.int32)
    return {
        'x': x,
        'mem': mem,
        'positions': positions,
        'norm_mix_pre': gain((L, D)),
        'norm_mix_post': gain((L, D)),
        'norm_xattn_pre': gain((L, D)),
        'norm_xattn_post': gain((L, D)),
        'norm_mem': gain((L, D)),
        'norm_mlp_pre': gain((L, D)),
        'norm_mlp_post': gain((L, D)),
        'w_in': dense((L, D, IN_COLS), D),
        'rw_mu': unif((L, RW_COLS), 0.0, 1.0),
        'rw_w0': unif((L, RW_WIDTH), -6.0, -1.0),
        'rw_w_up': dense((L, RW_DECAY_LORA, RW_WIDTH), RW_DECAY_LORA, 0.5),
        'rw_a0': noise((L, RW_WIDTH), 0.1),
        'rw_a_up': dense((L, RW_AAA_LORA, RW_WIDTH), RW_AAA_LORA),
        'rw_g_up': dense((L, RW_GATE_LORA, RW_WIDTH), RW_GATE_LORA),
        'rw_k_k': 0.85 + noise((L, RW_WIDTH), 0.02),
        'rw_k_a': 1.0 + noise((L, RW_WIDTH), 0.02),
        'rw_r_k': noise((L, RW_HEADS, HEAD_DIM), 0.1),
        'rw_lnx_w': gain((L, RW_WIDTH)),
        'rw_lnx_b': noise((L, RW_WIDTH), 0.01),
        'rw_vres_down': dense((L - 1, D, RW_MV_LORA), D),
        'rw_vres_mu': unif((L - 1, RW_MV_LORA), 0.0, 1.0),
        'rw_v0': 1.0 + noise((L - 1, RW_WIDTH), 0.1),
        'rw_vres_up': dense((L - 1, RW_MV_LORA, RW_WIDTH), RW_MV_LORA),
        'sw_sinks': noise((L, SW_Q_HEADS), 1.0),
        'w_branch': dense((L, N_BRANCH, BRANCH_WIDTH, D), BRANCH_WIDTH),
        'w_out': dense((L, D, D), D),
        'w_xq': dense((L, D, XA_WIDTH), D),
        'w_xk': dense((L, D, XA_WIDTH), D),
        'w_xv': dense((L, D, XA_WIDTH), D),
        'w_xo': dense((L, XA_WIDTH, D), XA_WIDTH),
        'w_up': dense((L, D, D_FF), D),
        'w_down': dense((L, D_FF, D), D_FF),
    }

def reference(x, mem, positions, norm_mix_pre, norm_mix_post, norm_xattn_pre, norm_xattn_post,
              norm_mem, norm_mlp_pre, norm_mlp_post, w_in, rw_mu, rw_w0, rw_w_up, rw_a0, rw_a_up,
              rw_g_up, rw_k_k, rw_k_a, rw_r_k, rw_lnx_w, rw_lnx_b, rw_vres_down, rw_vres_mu, rw_v0,
              rw_vres_up, sw_sinks, w_branch, w_out, w_xq, w_xk, w_xv, w_xo, w_up, w_down):
    B, S, D = x.shape
    cos, sin = rope_tables(positions)
    col_splits = [RW_COLS, RW_COLS + MB_COLS, RW_COLS + MB_COLS + SW_COLS]
    v_first = None
    for l in range(DEPTH):
        h = rms_norm(x, norm_mix_pre[l])
        u = h @ w_in[l]
        u_rw, u_mb, u_sw, u_gate = jnp.split(u, col_splits, axis=-1)
        if l == 0:
            v_gate = None
        else:
            vm = token_shift_lerp(h @ rw_vres_down[l - 1], rw_vres_mu[l - 1])
            v_gate = jax.nn.sigmoid(rw_v0[l - 1] + vm @ rw_vres_up[l - 1])
        o_rw, v_rw = rwkv7_branch(u_rw, rw_mu[l], rw_w0[l], rw_w_up[l], rw_a0[l], rw_a_up[l],
                                  rw_g_up[l], rw_k_k[l], rw_k_a[l], rw_r_k[l], rw_lnx_w[l],
                                  rw_lnx_b[l], v_first, v_gate)
        if l == 0:
            v_first = v_rw
        mq, mk, mv = jnp.split(u_mb, 3, axis=-1)
        mq = apply_rope(mq.reshape(B, S, MB_HEADS, HEAD_DIM), cos, sin)
        mk = apply_rope(mk.reshape(B, S, MB_HEADS, HEAD_DIM), cos, sin)
        o_mb = moba_attention(mq, mk, mv.reshape(B, S, MB_HEADS, HEAD_DIM))
        sq, sk, sv = jnp.split(u_sw, [SW_WIDTH, SW_WIDTH + SW_KV_WIDTH], axis=-1)
        sq = apply_rope(sq.reshape(B, S, SW_Q_HEADS, HEAD_DIM), cos, sin)
        sk = apply_rope(sk.reshape(B, S, SW_KV_HEADS, HEAD_DIM), cos, sin)
        o_sw = swa_sink_attention(sq, sk, sv.reshape(B, S, SW_KV_HEADS, HEAD_DIM), sw_sinks[l])
        branches = jnp.stack([o_rw, o_mb, o_sw], axis=2)
        proj = jnp.einsum('bsnc,ncd->bsnd', branches, w_branch[l])
        gates = jax.nn.sigmoid(u_gate.reshape(B, S, N_BRANCH, D))
        y = jnp.sum(gates * proj, axis=2) @ w_out[l]
        x = x + rms_norm(y, norm_mix_post[l])
        h = rms_norm(x, norm_xattn_pre[l])
        m = rms_norm(mem, norm_mem[l])
        xa = memory_cross_attention(h, m, w_xq[l], w_xk[l], w_xv[l], w_xo[l])
        x = x + rms_norm(xa, norm_xattn_post[l])
        h = rms_norm(x, norm_mlp_pre[l])
        x = x + rms_norm(squared_relu_mlp(h, w_up[l], w_down[l]), norm_mlp_post[l])
    return x


_drawn_inputs = setup_inputs


def setup_inputs(seed=0):
    import zlib

    import numpy as np

    out = dict(_drawn_inputs(seed))
    spreads = {}
    factors = {'norm_mix_post': 3.02,
     'norm_xattn_pre': 3.416,
     'norm_xattn_post': 3.333,
     'norm_mlp_pre': 3.693,
     'norm_mlp_post': 4.028,
     'rw_k_k': 4.239,
     'rw_k_a': 3.245,
     'rw_lnx_w': 3.933,
     'rw_lnx_b': 6.165,
     'rw_v0': 43.944,
     'sw_sinks': 4.879,
     'rw_vres_down': 8.0,
     'rw_vres_mu': 8.0,
     'rw_vres_up': 8.0}
    for name, (base, spread) in spreads.items():
        noise = np.random.default_rng([zlib.crc32(name.encode()), seed]).standard_normal(out[name].shape)
        drawn = base * np.exp(spread * noise) if base else spread * noise
        out[name] = jnp.asarray(drawn.astype(out[name].dtype))
    for name, factor in factors.items():
        out[name] = (out[name] * factor).astype(out[name].dtype)
    return out
```

```python
import math
from contextlib import ExitStack

import numpy as np

import concourse.bass as bass
import concourse.mybir as mybir
from concourse.alu_op_type import AluOpType as ALU

ACT = mybir.ActivationFunctionType
AX = mybir.AxisListType
F32 = mybir.dt.float32
F32R = mybir.dt.float32r
I32 = mybir.dt.int32

P = 128
D = 1024
SEQ = 256
DEPTH = 2
MEM = 256
HD = 64
HEADS = 8
WIDTH = HEADS * HD
PAIRS = HEADS // 2
CHUNK = 64
CHUNKS = SEQ // CHUNK
TT = SEQ // P
KT = D // P
COLS = 512
D_FF = 4096
XH = 4
XD = 128
WINDOW = 128
ROPE_THETA = 10000.0
NORM_EPS = 1e-6
LNX_EPS = 1e-5 * HD
MASK = -1e30
UNIT = 2048
LOGW = -0.5 * math.exp(-0.5)
ROUND = 1.5 * 2.0 ** 23


def _two_pi_parts():
    rest, parts = 2 * math.pi, []
    for _ in range(4):
        m, e = math.frexp(rest)
        part = math.ldexp(math.floor(m * 1024), e - 10)
        parts.append(part)
        rest -= part
    return parts


TWO_PI_PARTS = _two_pi_parts()

C_R, C_K, C_V, C_LORA = 0, 512, 1024, 1536
C_MQ, C_MK, C_MV = 1792, 2304, 2816
C_SQ, C_SKV, C_GATE = 3328, 3840, 4096

PROWS = [("mix_pre", 8), ("xattn_pre", 8), ("mlp_pre", 8), ("mem", 8), ("mu", 14), ("w0", 4), ("a0", 4),
         ("k_k", 4), ("k_a", 4), ("r_k", 4), ("lnx_w", 4), ("lnx_b", 4), ("v0", 4)]
PROW_AT = {}
NPROW = 0
for _name, _n in PROWS:
    PROW_AT[_name] = NPROW
    NPROW += _n

CONST_COLS = [("ident", 128), ("cmask", 128), ("level", 6 * 64), ("amask", 640), ("blk", 128),
              ("sel8", 32), ("ident2", 64), ("selT8", 512), ("invf", 32)]
CONST_AT = {}
NCONST = 0
for _name, _n in CONST_COLS:
    CONST_AT[_name] = (NCONST, _n)
    NCONST += _n

GEMMS = [("lora", "T", 1, "act"), ("skv", "N", 1, "dve"),
         ("k", "T", 2, "act"), ("v", "T", 2, "act"), ("r", "T", 2, "act"),
         ("mq", "N", 2, "dve"), ("mk", "N", 2, "dve"), ("mv", "N", 2, "act")]
for _b in (1, 2, 0):
    GEMMS += [(f"gate{_b}{_h}", "N", 2, "act") for _h in (0, 1)]
    if _b == 1:
        GEMMS.append(("sq", "N", 2, "dve"))
    GEMMS += [(f"branch{_b}{_h}", "N", 1, "dve") for _h in (0, 1)]
GEMMS += [("xk", "T", 2, "act"), ("out0", "N", 2, "dve"), ("out1", "N", 2, "dve"), ("xv", "N", 2, "act"), ("xq", "T", 2, "act"),
          ("xo0", "N", 1, "dve"), ("xo1", "N", 1, "dve")]
GEMMS += [(f"up{_h}", "N", 2, "dve") for _h in range(8)]
GEMMS += [("down", "D", 16, "dve")]
KIND = {g[0]: g[1] for g in GEMMS}
TAKER = {g[0]: g[3] for g in GEMMS}
FIRST_UNIT, N_UNITS, BANK0 = {}, {}, {}
_at = 0
for _i, (_name, _o, _n, _t) in enumerate(GEMMS):
    FIRST_UNIT[_name], N_UNITS[_name], BANK0[_name] = _at, _n, 2 * (_i % 2)
    _at += _n
BANK0["down"] = 0
NW = _at
RING = 4
HIGH = 3
assert NW % HIGH == 0


POST_AFTER = ["out1", "xo1", "down"]
POST_HALVES = {"out0": (0,), "out1": (1,), "xo0": (0,), "xo1": (1,), "down": (0, 1)}
N_PARAMS = len(PROWS)
N_LORAS = 7


def taken_count(name):
    n = 0
    for g, _, _, taker in GEMMS:
        if taker == TAKER[name]:
            n += 2 if g == "down" else 1
        if g == name:
            return n


def before_in_banks(name):
    names = [g[0] for g in GEMMS]
    i = names.index(name)
    if name == "down":
        return names[i - 2:i]
    return names[i - 2:i - 1] if i >= 2 else []


def pieces(name):
    n = N_UNITS[name]
    if name == "down":
        return 16
    if name in ("mk", "mv", "gate10", "gate11"):
        return 8
    return 2 if n == 1 else 4


def gemm_pieces(*names):
    return [("gemm", n, q) for n in names for q in range(pieces(n))]


def mix(long, *shorts):
    out, at = [], [0] * len(shorts)
    for i, piece in enumerate(long):
        out.append(piece)
        windows = []
        for s, short in enumerate(shorts):
            until = (i + 1) * len(short) // len(long)
            windows.append(short[at[s]:until])
            at[s] = until
        for turn in range(max(map(len, windows), default=0)):
            out += [w[turn] for w in windows if turn < len(w)]
    return out


def attention(b, long, state):
    long, state, out = list(long), list(state), []
    per_pair, per_long = -(-len(state) // PAIRS), -(-len(long) // PAIRS)

    def some(of, n):
        taken_now = of[:n]
        del of[:n]
        return taken_now

    for pair in range(PAIRS):
        out += [("scores", b, pair)] + some(long, -(-per_long // 2)) + some(state, 1) + [("pT", b, pair)]
        out += some(state, per_pair - 2) + some(long, per_long // 2) + [("pv", b, pair)] + some(state, 1)
    return out + [("oT", b)] + state + long


LEVELS = 6
STATE = [(s, c) for c in range(CHUNKS) for s in ("chunk_m", "chunk_x", "chunk_sa", "chunk_o", "chunk_z")]
CROSS = [("xscores", 0)] + [s for h in range(XH) for s in [("xscores", h + 1)] * (h == 0) + [("xpT", h), ("xpv", h)]
                            + [("xscores", h + 2)] * (h + 2 < XH)]
NORM_OUT = [("gn_mean", 0), ("gn_var", 0), ("gn_T", 0), ("gn_scale", 0), ("rw_high", 0), ("rw_low", 0)]
_long = gemm_pieces("mk", "mv", "gate10", "gate11")
MERGING = [("v_token", 0), _long.pop(0), ("bk_token", 0), _long.pop(0), ("low", 0), _long.pop(0), _long.pop(0)]
for _n in range(LEVELS):
    MERGING += [("merge_p", _n), _long.pop(0), ("merge_u", _n)]
    if _n < LEVELS - 1:
        MERGING += ([_long.pop(0)] if _n >= 2 else []) + [("merge_l", _n), _long.pop(0)]
MERGING.append(_long.pop(0))
PIECES_UP = [2] * 7 + [4]
STAGES = (
    [("params", 0), ("pre_scale", 0), ("pre_T", 0)]
    + gemm_pieces("lora") + [("v_down", 0), ("lora_tanh", 0)] + gemm_pieces("skv") + [("vres_down", 0), ("lora_sig", 0)]
    + mix(gemm_pieces("k"), [("lora_up", 0), ("decay", 0), ("lora_g", 0)]) + [("k_in", 0)]
    + gemm_pieces("v") + [("kk_sum", 0), ("v_in", 0)]
    + mix(gemm_pieces("r"), [("kk_T", 0), ("fold_k", 0), ("kk_scale", 0), ("vres_up", 0)]) + [("v_gate", 0), ("fold", 0), ("r_in", 0)]
    + gemm_pieces("mq")[:3] + [("bonus", 0), ("zero", 0)] + gemm_pieces("mq")[3:]
    + MERGING
    + [("trq", 1), ("trk", 1)] + attention(1, _long, STATE[0:10])
    + gemm_pieces("sq") + mix(gemm_pieces("branch10", "branch11"), STATE[10:12]) + [("trq", 2), ("trk", 2)]
    + attention(2, gemm_pieces("gate20", "gate21"), STATE[12:20])
    + mix(gemm_pieces("branch20", "branch21", "gate00"), NORM_OUT) + [("mem_scale", 0)] + gemm_pieces("gate01") + [("mem_T", 0)]
    + gemm_pieces("branch00", "branch01") + gemm_pieces("xk")[:1] + [("yT", 0)] + gemm_pieces("xk")[1:]
    + gemm_pieces("out0", "out1", "xv")
    + [("pre_T", 1), ("pre_scale", 1)] + gemm_pieces("xq")
    + CROSS + [("xoT", 0)]
    + gemm_pieces("xo0", "xo1") + [("pre_T", 2), ("pre_scale", 2)]
    + gemm_pieces("up0")
    + [s for h in range(1, 8) for s in gemm_pieces(f"up{h}")[:PIECES_UP[h]] + [("hiddenT", h - 1)]
       + gemm_pieces(f"up{h}")[PIECES_UP[h]:]]
    + gemm_pieces("down")[:2] + [("hiddenT", 7)] + gemm_pieces("down")[2:]
)

def with_splits(stages):
    out, due = [], {}
    piece = 0
    for stage in stages:
        if stage[0] == "gemm":
            out += due.pop(piece, [])
        out.append(stage)
        if stage == ("pre_scale", 0):
            out += [("split_high", 0), ("split_low", 0)]
        if stage == ("pre_T", 0):
            out += [(part, u) for u in range(1, HIGH) for part in ("split_high", "split_low")]
        if stage[0] == "gemm":
            _, name, q = stage
            per_unit = pieces(name) // N_UNITS[name]
            u = FIRST_UNIT[name] + q // per_unit + HIGH
            if q % per_unit == per_unit - 1 and u < NW:
                due.setdefault(piece + 1, []).append(("split_high", u))
                due.setdefault(piece + 2, []).append(("split_low", u))
            piece += 1
    assert not due
    return out


ORDER = with_splits(STAGES)

SHORT = {"params": ([4], "dve"), "pre_T": ([4, 5, 6, 7], "dve"), "vres_down": ([4], "act"),
         "lora_up": ([4, 5, 6, 7], "act"), "lora_g": ([4, 5], "act"), "kk_sum": ([6], "dve"), "kk_T": ([6], "dve"),
         "kk_scale": ([4, 5], "dve"), "vres_up": ([6, 7], "act"), "v_token": ([4, 5, 6, 7], "act"),
         "bonus": ([4, 5], "dve"), "bk_token": ([4, 5, 6, 7], "act"), "low": ([4, 5], "act"),
         "merge_p": ([4, 5], "act"), "merge_u": ([6, 7], "dve"), "merge_l": ([4, 5], "dve"), "chunk_m": ([4, 5], "dve"),
         "chunk_x": ([4], "act"), "chunk_sa": ([5], "act"), "chunk_o": ([4], "act"), "chunk_z": ([5], "dve"),
         "gn_mean": ([4, 5], "dve"), "gn_var": ([4], "dve"), "gn_T": ([4], "dve"), "gn_scale": ([4, 5], "dve"),
         "trq": ([6, 7], "act"), "trk": ([6, 7], "act"), "scores": ([6, 7], "dve"), "pT": ([6, 7], "dve"),
         "pv": ([6], "dve"), "oT": ([6, 7], "act"), "yT": ([4, 5, 6, 7], "act"), "xscores": ([4, 5], "act"),
         "xpT": ([6, 7], "dve"), "xpv": ([4, 5], "dve"), "xoT": ([6, 7], "act"), "hiddenT": ([4, 5, 6, 7], "act"), "mem_T": ([4, 5, 6, 7], "dve")}


def constants():
    c = np.zeros((P, NCONST), np.float32)

    def put(name, a):
        at, n = CONST_AT[name]
        c[:a.shape[0], at:at + n] = a.reshape(a.shape[0], n)

    p = np.arange(P)[:, None]
    put("ident", np.eye(P, dtype=np.float32))
    s, t = p % CHUNK, np.arange(P)[None, :]
    put("cmask", np.where(t < CHUNK, s < t, s <= t - CHUNK).astype(np.float32))
    col = np.arange(CHUNK)[None, :]
    row = p % CHUNK
    level = [(row // (2 * n) == col // (2 * n)) & (row % (2 * n) >= n) & (col % (2 * n) < n)
             for n in (1, 2, 4, 8, 16, 32)]
    put("level", np.stack(level, 1).astype(np.float32))
    q, k = p, np.arange(P)[None, :]
    causal = np.where(k <= q, 0.0, MASK)
    band = np.where(P + q - k < WINDOW, 0.0, MASK)
    put("amask", np.concatenate([causal, np.zeros((P, P)), causal, band, causal], 1).astype(np.float32))
    put("blk", (p // HD == np.arange(P)[None, :] // HD).astype(np.float32))
    head_of = 2 * np.arange(PAIRS)[None, :] + p // HD
    sel = (head_of[:, :, None] == np.arange(HEADS)[None, None, :]).astype(np.float32)
    put("sel8", sel)
    put("ident2", (row == col).astype(np.float32))
    put("selT8", np.ascontiguousarray(sel.transpose(2, 1, 0)))
    inv = 1.0 / (ROPE_THETA ** (np.arange(0, HD, 2, dtype=np.float32) / np.float32(HD)))
    put("invf", np.broadcast_to(inv.astype(np.float32), (P, HD // 2)))
    return c


INVF_AT = CONST_AT["invf"][0]
assert INVF_AT + HD // 2 == NCONST


class Counts:

    def __init__(self):
        self.n = {}

    def __call__(self, signal):
        self.n[signal] = self.n.get(signal, 0) + 1
        return self.n[signal]


def build(nc, t, out):
    ctx = ExitStack()
    with ctx:
        def sb(name, shape, dt=F32):
            return ctx.enter_context(nc.sbuf_tensor(name, shape, dt))

        def split_twin(name, shape):
            return nc.alloc_sbuf_tensor_at(name, shape, F32R, offset=nc.sbuf_base - 4 * int(np.prod(shape[1:])))

        F = PAIRS * SEQ

        ring = sb("ring", [P, RING, UNIT])
        ring_low = split_twin("ring_low", [P, RING, UNIT])
        high = sb("high", [P, HIGH, UNIT], F32R)
        x = sb("x", [P, TT, D])
        cst = sb("cst", [P, NCONST])
        prow = sb("prow", [NPROW, P])
        pcol = sb("pcol", [P, NPROW])
        half = sb("half", [P, 20])
        cos = sb("cos", [P, TT, HD // 2])
        sin = sb("sin", [P, TT, HD // 2])
        sinks = sb("sinks", [P, HEADS])
        lora_up = sb("lora_up", [P, WIDTH])
        g_up = sb("g_up", [P, WIDTH])
        v_up = sb("v_up", [32, WIDTH])
        v_down = sb("v_down", [P, KT, 32])
        v_down_low = split_twin("v_down_low", [P, KT, 32])
        v_down_high = sb("v_down_high", [P, KT, 32], F32R)
        v_mu = sb("v_mu", [32, 1])
        not_first = sb("not_first", [P, 1])
        neg_half = sb("neg_half", [P, TT * HEADS])
        stat = sb("stat", [P, 24])
        soft = sb("soft", [P, 40])
        v_first = sb("v_first", [P, PAIRS, SEQ])
        hT = sb("hT", [P, KT, SEQ], F32R)
        hT_low = sb("hT_low", [P, KT, SEQ], F32R)
        pbuf = sb("pbuf", [P, 4 * 384])
        pend = sb("pend", [P, PAIRS, CHUNKS])
        pos = sb("pos", [P, TT], I32)
        gates = sb("gates", [P, 2, TT, COLS])
        oT = sb("oT", [P, PAIRS, SEQ], F32R)
        BIG = 16388 + 3 * F + 768 + 2 * F
        big = sb("big", [P, BIG])
        big_split = split_twin("big_split", [P, BIG])

        def cut(at, *shape, of=big):
            n = int(np.prod(shape))
            assert at + n <= BIG, at + n
            v = of[:, at:at + n]
            if len(shape) == 2:
                return v.rearrange("p (a b) -> p a b", b=shape[1])
            if len(shape) == 3:
                return v.rearrange("p (a b c) -> p a b c", b=shape[1], c=shape[2])
            return v

        def cut_split(at, *shape):
            return cut(at, *shape, of=big_split)

        AR = cut(0, PAIRS, CHUNKS, P)
        BK = cut(2 * F, PAIRS, CHUNKS, P)
        SV = cut(4 * F, PAIRS, CHUNKS, P)
        TMP = cut(4 * F, PAIRS, SEQ)
        KK = cut(5 * F, PAIRS, SEQ)
        BON = cut(6 * F, PAIRS, SEQ)
        U = cut(6 * F, PAIRS, SEQ + 1)
        G = cut(7 * F + 4, PAIRS, SEQ)
        E0 = 8 * F + 4
        Ks = cut(E0, PAIRS, SEQ)
        Rs = cut(E0 + F, PAIRS, SEQ)
        VT = cut(E0 + 2 * F, PAIRS, CHUNK + SEQ)
        A1 = cut(E0 + 3 * F + 256, PAIRS, SEQ)
        A2 = cut(E0 + 4 * F + 256, PAIRS, SEQ)
        A3 = cut(E0 + 5 * F + 256, PAIRS, SEQ)
        TA = cut(E0 + 6 * F + 256, PAIRS, SEQ)
        V = VT[:, :, CHUNK:CHUNK + SEQ]
        BKt = cut(E0, PAIRS, CHUNKS, P)
        Nl = cut(E0 + 2 * F, HEADS, 2, CHUNK)
        El = cut(E0 + 3 * F, HEADS, 2, CHUNK)
        Tu = cut(E0 + 4 * F, HEADS, 2, CHUNK)
        Tl = cut(E0 + 5 * F, HEADS, 2, CHUNK)
        P1 = cut(E0 + 6 * F, HEADS, 2, CHUNK)
        MC = cut(E0 + 5 * F, 2, HEADS, P)
        Z = cut(E0 + 7 * F, PAIRS, P)
        XS = cut(E0 + 7 * F + 512, WIDTH)
        S8b, R8b, R8bT = XS[:, 0:16], XS[:, 16:32], XS[0:HEADS, SEQ:2 * SEQ]
        OT = cut(E0 + 2 * F, PAIRS, SEQ)
        OSQ = cut(E0 + 3 * F, PAIRS, SEQ)
        RWO = OSQ
        RWO_low, RWO_high = cut_split(E0 + 3 * F, PAIRS, SEQ), cut_split(E0 + 4 * F, PAIRS, SEQ)
        E1 = E0 + 8 * F
        QTOK = cut(E1, TT, WIDTH)
        QT = cut(E1 + F, PAIRS, SEQ)
        KTt = cut(E1 + 2 * F, PAIRS, SEQ)
        oT_low = cut_split(E1 + F, PAIRS, SEQ)
        SKTOK = cut(E1 + 3 * F, TT, 256)
        SVTOK = cut(E1 + 3 * F + 512, TT, P)
        E2 = E1 + 3 * F + 768
        ACC = cut(E2, TT, D)
        VTOK = cut(E2, TT, WIDTH)
        KTOK = cut(E2 + F, TT, WIDTH)
        VG, VD = cut(E2, PAIRS, SEQ), cut(E2 + F, PAIRS, SEQ)
        hrow = ACC
        mem_rows = cut(2 * F, TT, D)
        mT_low, mT_high = cut_split(E1, KT, MEM), cut_split(5 * F, KT, MEM)
        pflat, qflat = pbuf[:, 0:768], pbuf[:, 768:1536]
        probs, probsT = (f.rearrange("p (h k) -> p h k", h=2) for f in (pflat, qflat))
        RSCR = pbuf[:, 0:1024]
        gflat = gates[:, :, :, :].rearrange("p a b c -> p (a b c)")
        post_gain = gflat[:, 0:D]
        TWA, SG = pflat[:, 0:SEQ], pflat[:, SEQ:2 * SEQ]
        S8, R8 = pflat[:, 2 * SEQ:2 * SEQ + 16], pflat[:, 2 * SEQ + 16:2 * SEQ + 32]
        VM, R8T, LTMP = qflat[:, 0:SEQ], qflat[0:HEADS, SEQ:2 * SEQ], qflat[:, 2 * SEQ:3 * SEQ]
        U2 = gflat[:, 0:2 * (SEQ + 1)].rearrange("p (a b) -> p a b", b=SEQ + 1)
        UV = gflat[0:32, 520:520 + SEQ + 1]
        XS2 = gflat[:, 800:800 + 2 * SEQ].rearrange("p (a b) -> p a b", b=SEQ)
        RESET = gflat[:, 1312:1312 + SEQ]
        YT, YT_low = cut_split(0, KT, SEQ), cut_split(2 * F, KT, SEQ)
        XQT = cut(4 * F, XH, SEQ)
        XP = cut(5 * F, 2, TT, MEM)
        XPT = cut(6 * F, 2, TT, SEQ)
        XO = cut(7 * F, TT, WIDTH)
        XOT, XOT_low = cut_split(8 * F, XH, SEQ), cut_split(9 * F, XH, SEQ)
        xkT = cut(10 * F, XH, MEM)
        xv = cut(11 * F, TT, WIDTH)
        HID, HID_low = cut_split(0, D_FF // P, SEQ), cut_split(8 * F, D_FF // P, SEQ)
        RELU = cut(E1, 2, TT, COLS)
        SQUARED = cut(E1 + 2 * F, PAIRS, SEQ)
        POST = cut(12 * F, TT, D)
        SQ = cut(14 * F, 2 * D)

        angle = cut(0, TT, HD // 2)
        turns = cut(64, TT, HD // 2)
        pos_f = cut(128, TT)

        psum = ctx.enter_context(nc.psum_tensor("psum", [P, 8, 512], F32))

        def con(name, *shape):
            at, n = CONST_AT[name]
            v = cst[:, at:at + n]
            if len(shape) == 2:
                return v.rearrange("p (a b) -> p a b", b=shape[1])
            return v

        ident, cmask, level = con("ident"), con("cmask"), con("level", LEVELS, CHUNK)
        blk, sel8, ident2 = con("blk"), con("sel8", PAIRS, HEADS), con("ident2")
        selT8, invf, am = con("selT8", PAIRS, P), con("invf"), con("amask")
        amask = {1: am[:, 0:384], 2: am[:, 256:640]}

        def pc(name, j=0, n=1):
            at = PROW_AT[name] + j
            return pcol[:, at:at + n]

        def sem(name):
            return ctx.enter_context(nc.semaphore(name))

        weights_loaded = [sem(f"weights_loaded_{i}") for i in range(RING)]
        weights_used = sem("weights_used")
        layer_end = sem("layer_end")
        layer_clear = sem("layer_clear")
        start_const, start_invf, start_x, start_pos = (sem(n) for n in ("start_const", "start_invf", "start_x",
                                                                        "start_pos"))
        start_link, pool_start, angles_ready, sines_ready = (sem(n) for n in ("dve_start_link", "pool_memsets",
                                                                              "angles_ready", "sines_ready"))
        post_gain_in, params_in, loras_in, mem_in = (sem(n) for n in ("post_gain_in", "params_in", "loras_in",
                                                                         "mem_in"))
        wait_carrier = sem("wait_carrier")
        stored = sem("stored")
        NAMES = {"pe": list(SHORT),
                 "act": [k for k, v in SHORT.items() if v[1] == "act"]
                 + ["gemm", "split_high", "pre_T", "mem_T", "mem_squares", "v_down", "rw_high", "squares", "lora_tanh",
                    "decay", "exps", "post_squares"],
                 "dve": [k for k, v in SHORT.items() if v[1] == "dve"]
                 + ["gemm", "split_low", "oT", "yT", "xoT", "hiddenT", "mem_scale", "v_down", "rw_low", "pre_scale",
                    "lerp", "lora_lerp", "lora_sig", "vres_lerp", "scan", "kk", "fold", "bonus_in", "rw_o", "rope",
                    "xmax", "post"],
                 "pool": ["rstd", "kk_sq", "kk_pow", "mask", "gn_sq", "gn_pow", "post_rstd", "zero", "mem_rstd",
                          "v_done"]}
        pe_done, act_done, dve_done, pool_done = ({s: sem(f"{e}_{s}") for s in NAMES[e]}
                                                  for e in ("pe", "act", "dve", "pool"))
        act_link, dve_link, pool_link = (sem(f"{e}_link") for e in ("act", "dve", "pool"))
        per_layer = [s for e in (pe_done, act_done, dve_done, pool_done) for s in e.values()] \
            + [act_link, dve_link, pool_link]
        nums = sorted(s.num for s in per_layer)
        assert nums == list(range(nums[0], nums[0] + len(nums)))

        block = ctx.enter_context(nc.Block())

        def after(l, name):
            return l * NW + (RING + FIRST_UNIT[name] + N_UNITS[name])

        def slot_loads(u):
            return len(range(u % RING, NW, RING))

        def taken(name):
            return (act_done if TAKER[name] == "act" else dve_done)["gemm"], taken_count(name)

        def bank(b):
            return psum[:, b, :]

        def pair_tiles(b):
            return psum[:, b:b + 2, :].rearrange("p b (f s) -> p (b f) s", s=SEQ)

        IN_COLS = {"k": C_K, "v": C_V, "r": C_R, "mq": C_MQ, "mk": C_MK, "mv": C_MV, "sq": C_SQ}

        def source(l, name, i):
            def block_of(w, k0, kn, c0, cn):
                return w[k0 * P:(k0 + kn) * P, c0:c0 + cn].rearrange("(t p) n -> p t n", p=P)
            if name in IN_COLS:
                return block_of(t["w_in"][l], 4 * i, 4, IN_COLS[name], COLS)
            if name == "lora":
                return block_of(t["w_in"][l], 0, 8, C_LORA, 256)
            if name == "skv":
                return block_of(t["w_in"][l], 0, 8, C_SKV, 256)
            if name[:4] == "gate":
                return block_of(t["w_in"][l], 4 * i, 4, C_GATE + int(name[4]) * D + int(name[5]) * COLS, COLS)
            if name[:6] == "branch":
                return block_of(t["w_branch"][l, int(name[6])], 0, 4, int(name[7]) * COLS, COLS)
            if name[:3] == "out":
                return block_of(t["w_out"][l], 4 * i, 4, int(name[3]) * COLS, COLS)
            if name in ("xq", "xk", "xv"):
                return block_of(t["w_" + name][l], 4 * i, 4, 0, COLS)
            if name[:2] == "xo":
                return block_of(t["w_xo"][l], 0, 4, int(name[2]) * COLS, COLS)
            if name[:2] == "up":
                return block_of(t["w_up"][l], 4 * i, 4, int(name[2]) * COLS, COLS)
            return block_of(t["w_down"][l], 2 * i, 2, 0, D)

        def parameters(l):
            rows = {"mix_pre": t["norm_mix_pre"][l], "xattn_pre": t["norm_xattn_pre"][l],
                    "mlp_pre": t["norm_mlp_pre"][l], "mem": t["norm_mem"][l], "mu": t["rw_mu"][l],
                    "w0": t["rw_w0"][l], "a0": t["rw_a0"][l], "k_k": t["rw_k_k"][l], "k_a": t["rw_k_a"][l],
                    "r_k": t["rw_r_k"][l].rearrange("h n -> (h n)"), "lnx_w": t["rw_lnx_w"][l],
                    "lnx_b": t["rw_lnx_b"][l], "v0": t["rw_v0"][0]}
            return [(prow[PROW_AT[name]:PROW_AT[name] + n, :], rows[name].rearrange("(r c) -> r c", c=P), params_in)
                    for name, n in PROWS] + [
                (dst, src, loras_in) for dst, src in (
                    (lora_up[0:64, :], t["rw_w_up"][l]), (lora_up[64:128, :], t["rw_a_up"][l]),
                    (g_up[:, :], t["rw_g_up"][l]), (v_up[:, :], t["rw_vres_up"][0]),
                    (v_down[:, :, :], t["rw_vres_down"][0].rearrange("(t p) n -> p t n", p=P)),
                    (v_mu[:, :], t["rw_vres_mu"][0].rearrange("(n a) -> n a", a=1)),
                    (sinks[:, :], t["sw_sinks"][l].partition_broadcast(P)))]

        @block.sync
        def _(sp):
            assert DEPTH == 2
            next_parameters = parameters(DEPTH - 1)
            first = FIRST_UNIT["up1"]
            sp.dma_start(x[:, :, :], t["x"][0].rearrange("(t p) n -> p t n", p=P)).then_inc(start_x, 16)
            sp.dma_start(cst[:, 0:INVF_AT], t["consts"][:, 0:INVF_AT]).then_inc(start_const, 16)
            with sp.Fori(0, DEPTH) as l:
                w = 0
                for name, _, n, _ in GEMMS:
                    for i in range(n):
                        before = w - RING if w >= RING else NW - 1 - (NW - 1 - w) % RING - NW
                        sp.wait_ge(weights_used, l * NW + (RING + before + 1))
                        sp.sem_inc(wait_carrier, 1)
                        src = source(l, name, i)
                        sp.dma_start(ring[:, w % RING, :].rearrange("p (t n) -> p t n", n=src.shape[2]),
                                     src).then_inc(weights_loaded[w % RING], 16)
                        if w == first:
                            sp.wait_ge(dve_done["pre_T"], 3 * KT)
                        if first <= w < first + len(next_parameters):
                            dst, src, loaded = next_parameters[w - first]
                            sp.dma_start(dst, src).then_inc(loaded, 16)
                        w += 1
            sp.wait_ge(layer_clear, DEPTH)
            sp.dma_start(out[0].rearrange("(t p) n -> p t n", p=P), x[:, :, :]).then_inc(stored, 16)
            sp.wait_ge(params_in, (DEPTH + 1) * 16 * N_PARAMS)
            sp.wait_ge(loras_in, (DEPTH + 1) * 16 * N_LORAS)
            sp.wait_ge(stored, 16)

        @block.tensor
        def _(pe):
            mm = nc.tensor.matmul

            def to_features(rows):
                for k in range(KT):
                    for m in range(TT):
                        at = (k % 2) * SEQ + m * P
                        last = nc.tensor.transpose(psum[:, 4 + k // 2, at:at + P], rows[:, m, k * P:(k + 1) * P], ident)
                return last

            pe.wait_ge(start_const, 16)
            for _ in range(RING):
                pe.drain().then_inc(weights_used, 1)

            with pe.Fori(0, DEPTH) as l:
                streams = {}

                def unit(name, i):
                    w = FIRST_UNIT[name] + i
                    pe.wait_ge(dve_done["split_low"], w + 1)
                    return high[:, w % HIGH, :], ring_low[:, w % RING, :]

                def product(dst, left, right, start, stop):
                    mm(dst, left[0], right[0], start=start, stop=False)
                    mm(dst, left[0], right[1], start=False, stop=False)
                    return mm(dst, left[1], right[0], start=False, stop=stop)


                def part(pair, *at):
                    return tuple(side[at] for side in pair)

                def ready(name):
                    if name == "xk":
                        pe.wait_ge(dve_done["mem_T"], 1)
                    elif name == "branch00":
                        pe.wait_ge(dve_done["rw_low"], 1)
                    elif name == "down":
                        pe.wait_ge(dve_done["hiddenT"], 6)
                    for before in before_in_banks(name):
                        pe.wait_ge(*taken(before))

                def operand(name):
                    if name in ("xk", "xv"):
                        return mT_high, mT_low
                    if name[:7] == "branch0":
                        return RWO_high, RWO_low
                    if name[:6] == "branch":
                        return oT, oT_low
                    if name[:3] == "out":
                        return YT, YT_low
                    if name[:2] == "xo":
                        return XOT, XOT_low
                    return hT, hT_low

                def ready_row(name, k):
                    if name == "branch10":
                        pe.wait_ge(dve_done["oT"], k // 2 + 1)
                    elif name == "branch20":
                        pe.wait_ge(dve_done["oT"], 2 + k // 2 + 1)
                    elif name == "out0":
                        pe.wait_ge(dve_done["yT"], k // 2 + 1)
                    elif name == "xo0":
                        pe.wait_ge(dve_done["xoT"], k // 2 + 1)
                    elif name in ("lora", "xq", "up0"):
                        pe.wait_ge(dve_done["pre_T"], ("lora", "xq", "up0").index(name) * KT + k + 1)

                ALL = slice(None)

                def token_major(name):
                    n_units, b0, act_T = N_UNITS[name], BANK0[name], operand(name)
                    ready(name)
                    width = 256 if name == "skv" else COLS
                    kn = 4 if name[:6] == "branch" or name[:2] == "xo" else KT
                    per_unit = kn // n_units
                    for k in range(kn):
                        row = k % per_unit
                        ready_row(name, k)
                        if row == 0:
                            w = unit(name, k // per_unit)
                        for m in range(TT):
                            dst = psum[:, b0, m * 256:m * 256 + 256] if name == "skv" else bank(b0 + m)
                            shared = name == "skv"
                            last = product(dst, part(act_T, ALL, k, slice(m * P, (m + 1) * P)),
                                           part(w, ALL, slice(row * width, (row + 1) * width)),
                                           k == 0 and not (shared and m), k == kn - 1 and (not shared or m == 1))
                        if row == per_unit - 1:
                            last.then_inc(weights_used, 1)
                        if (k + 1) % (kn // pieces(name)) == 0:
                            yield

                def feature_major(name):
                    n_units, b0, act_T = N_UNITS[name], BANK0[name], operand(name)
                    ready(name)
                    width = 256 if name == "lora" else COLS
                    tiles = width // P
                    per_unit = KT // n_units
                    for k in range(KT):
                        row = k % per_unit
                        ready_row(name, k)
                        if row == 0:
                            w = unit(name, k // per_unit)
                        for f in range(tiles):
                            at = row * width + f * P
                            last = product(psum[:, b0 + f // 2, (f % 2) * 256:(f % 2) * 256 + 256],
                                           part(w, ALL, slice(at, at + P)), part(act_T, ALL, k, ALL),
                                           k == 0 and f % 2 == 0, k == KT - 1 and f % 2 == 1)
                        if row == per_unit - 1:
                            last.then_inc(weights_used, 1)
                        if (k + 1) % (KT // pieces(name)) == 0:
                            yield

                def down(name):
                    ready(name)
                    for i in range(N_UNITS[name]):
                        w = unit(name, i)
                        for row in range(2):
                            k = 2 * i + row
                            if k in (6 * PAIRS, 7 * PAIRS):
                                pe.wait_ge(dve_done["hiddenT"], k // PAIRS + 1)
                            for m in range(TT):
                                for h in range(2):
                                    last = product(bank(2 * h + m), part((HID, HID_low), ALL, k, slice(m * P, (m + 1) * P)),
                                                   part(w, ALL, slice(row * D + h * COLS, row * D + (h + 1) * COLS)),
                                                   k == 0, k == D_FF // P - 1)
                        last.then_inc(weights_used, 1)
                        yield

                def gemm(name, q):
                    if q == 0:
                        streams[name] = {"N": token_major, "T": feature_major, "D": down}[KIND[name]](name)
                    next(streams[name])

                def params(_):
                    pe.wait_ge(params_in, (l + 1) * (16 * N_PARAMS))
                    return nc.tensor.transpose(psum[:, 4, 0:NPROW], prow[:, :], ident[0:NPROW, 0:NPROW])

                def pre_T(n):
                    if n == 0:
                        pe.wait_ge(dve_done["params"], 1)
                    else:
                        pe.wait_ge(dve_done[("yT", "xoT")[n - 1]], (4, 2)[n - 1])
                    if n == 0:
                        pe.wait_ge(dve_done["pre_scale"], 1)
                        return to_features(hrow)
                    pe.wait_ge(dve_done["post"], n)
                    return to_features(x)

                def mem_T(_):
                    pe.wait_ge(dve_done["rw_o"], 1)
                    pe.wait_ge(dve_done["oT"], 4)
                    pe.wait_ge(dve_done["mem_scale"], 1)
                    return to_features(mem_rows)

                def vres_down(_):
                    pe.wait_ge(dve_done["pre_T"], KT)
                    pe.wait_ge(dve_done["v_down"], 1)
                    for k in range(KT):
                        last = product(psum[0:32, 4, 0:SEQ], (v_down_high[:, k, :], v_down_low[:, k, :]),
                                       (hT[:, k, :], hT_low[:, k, :]), k == 0, k == KT - 1)
                    return last

                def tiles(b, lhs, rhs):
                    for j in range(PAIRS):
                        last = mm(pair_tiles(b)[:, j, :], lhs(j), rhs(j), start=True, stop=True)
                    return last

                def lora_up_(_):
                    pe.wait_ge(act_done["vres_down"], 1)
                    pe.wait_ge(act_done["lora_tanh"], 1)
                    for j in range(PAIRS):
                        mm(pair_tiles(6)[:, j, :], lora_up[0:64, j * P:(j + 1) * P], TWA[0:64, :], start=True, stop=True)
                        last = mm(pair_tiles(4)[:, j, :], lora_up[64:128, j * P:(j + 1) * P], TWA[64:128, :],
                                  start=True, stop=True)
                    return last

                def lora_g(_):
                    pe.wait_ge(act_done["lora_up"], 1)
                    pe.wait_ge(dve_done["lora_sig"], 1)
                    return tiles(4, lambda j: g_up[:, j * P:(j + 1) * P], lambda j: SG)

                def head_sums(b, src):
                    for m in range(TT):
                        for j in range(PAIRS):
                            last = mm(psum[:, b, m * HEADS:(m + 1) * HEADS], src[:, j, m * P:(m + 1) * P], sel8[:, j, :],
                                      start=(j == 0), stop=(j == PAIRS - 1))
                    return last

                def rows_of_heads(b, src):
                    for m in range(TT):
                        last = nc.tensor.transpose(psum[0:HEADS, b, m * P:(m + 1) * P], src[:, m * HEADS:(m + 1) * HEADS],
                                                   ident)
                    return last

                def kk_sum(_):
                    pe.wait_ge(act_done["lora_up"], 1)
                    pe.wait_ge(pool_done["kk_sq"], 1)
                    return head_sums(6, TMP)

                def kk_T(_):
                    pe.wait_ge(dve_done["kk_sum"], 1)
                    pe.wait_ge(pool_done["kk_pow"], 1)
                    return rows_of_heads(6, R8)

                def kk_scale(_):
                    pe.wait_ge(act_done["lora_g"], 1)
                    pe.wait_ge(dve_done["kk_T"], 1)
                    return tiles(4, lambda j: selT8[0:HEADS, j, :], lambda j: R8T)

                def vres_up(_):
                    pe.wait_ge(dve_done["kk_T"], 1)
                    pe.wait_ge(dve_done["vres_lerp"], 1)
                    return tiles(6, lambda j: v_up[:, j * P:(j + 1) * P], lambda j: VM[0:32, :])

                def bonus(_):
                    pe.wait_ge(dve_done["kk_scale"], 1)
                    pe.wait_ge(dve_done["bonus_in"], 1)
                    return tiles(4, lambda j: blk, lambda j: TMP[:, j, :])

                def v_token(_):
                    pe.wait_ge(dve_done["bonus"], 1)
                    pe.wait_ge(act_done["vres_up"], 1)
                    pe.wait_ge(pool_done["v_done"], 1)
                    for j in range(PAIRS):
                        for c in range(CHUNKS):
                            last = nc.tensor.transpose(psum[:, 4 + j, c * P:(c + 1) * P],
                                                       VT[:, j, c * CHUNK:c * CHUNK + P], ident)
                    return last

                def bk_token(_):
                    pe.wait_ge(act_done["v_token"], 1)
                    pe.wait_ge(dve_done["fold"], 1)
                    for j in range(PAIRS):
                        for c in range(CHUNKS):
                            last = nc.tensor.transpose(psum[:, 4 + j, c * P:(c + 1) * P], BK[:, j, c, :], ident)
                    return last

                def low(_):
                    pe.wait_ge(act_done["bk_token"], 1)
                    for j in range(PAIRS):
                        for p in range(2):
                            for c in range(CHUNKS):
                                rows, q = slice(64 * p, 64 * p + 64), 64 * (c % 2)
                                at = (2 * j + c // 2) * CHUNK
                                last = mm(psum[q:q + 64, 4 + p, at:at + CHUNK], AR[rows, j, c, 0:CHUNK],
                                          BK[rows, j, c, 0:CHUNK], start=True, stop=True)
                    return last

                def products(b, lhs, rhs):
                    for j in range(PAIRS):
                        for p in range(2):
                            for c in range(CHUNKS):
                                rows = slice(64 * (c % 2), 64 * (c % 2) + 64)
                                at = (2 * j + c // 2) * CHUNK
                                last = mm(psum[rows, b + p, at:at + CHUNK], lhs[rows, 2 * j + p, c // 2, :],
                                          rhs[rows, 2 * j + p, c // 2, :], start=True, stop=True)
                    return last

                def merge_p(n):
                    pe.wait_ge(pool_done["mask"], n + 1)
                    if n:
                        pe.wait_ge(dve_done["merge_u"], n)
                        pe.wait_ge(dve_done["merge_l"], n)
                    return products(4, El, Tu)

                def merge_u(n):
                    pe.wait_ge(act_done["merge_p"], n + 1)
                    return products(6, Tl, P1)

                def merge_l(n):
                    return products(4, P1, Tl)

                def chunk_m(c):
                    if c == 0:
                        pe.wait_ge(dve_done["merge_u"], LEVELS)
                    else:
                        pe.wait_ge(act_done["chunk_o"], c)
                        pe.wait_ge(dve_done["chunk_z"], c)
                    for j in range(PAIRS):
                        for p in range(2):
                            rows = slice(64 * p, 64 * p + 64)
                            last = mm(psum[:, 4 + p, j * P:(j + 1) * P], BK[rows, j, c, :], AR[rows, j, c, :],
                                      start=True, stop=True)
                    return last

                def chunk_x(c):
                    pe.wait_ge(dve_done["chunk_m"], c + 1)
                    if c:
                        pe.wait_ge(dve_done["chunk_z"], c)
                    q = 64 * (c % 2)
                    for j in range(PAIRS):
                        mm(psum[q:q + 64, 4, j * P:(j + 1) * P], AR[:, j, c, 0:CHUNK], Z[:, j, :], start=True, stop=False)
                        for p in range(2):
                            at = j * P + p * HD
                            last = mm(psum[q:q + 64, 4, at:at + HD], MC[:, c % 2, 2 * j + p, 0:CHUNK],
                                      SV[:, j, c, p * HD:(p + 1) * HD], start=False, stop=(p == 1))
                    return last

                def chunk_sa(c):
                    pe.wait_ge(act_done["chunk_x"], c + 1)
                    rows = slice(64 * (c % 2), 64 * (c % 2) + 64)
                    for h in range(HEADS):
                        last = mm(psum[0:64, 5, h * HD:(h + 1) * HD], Tu[rows, h, c // 2, :],
                                  XS[rows, h * HD:(h + 1) * HD], start=True, stop=True)
                    return last

                def chunk_o(c):
                    pe.wait_ge(act_done["chunk_x"], c + 1)
                    pe.wait_ge(act_done["chunk_sa"], c + 1)
                    for j in range(PAIRS):
                        mm(psum[:, 4, j * CHUNK:(j + 1) * CHUNK], Z[:, j, :], AR[:, j, c, CHUNK:P], start=True, stop=False)
                        for p in range(2):
                            last = mm(psum[64 * p:64 * p + 64, 4, j * CHUNK:(j + 1) * CHUNK],
                                      SV[:, j, c, p * HD:(p + 1) * HD], MC[:, c % 2, 2 * j + p, CHUNK:P],
                                      start=False, stop=True)
                    return last

                def chunk_z(c):
                    for j in range(PAIRS):
                        for p in range(2):
                            last = mm(psum[64 * p:64 * p + 64, 5, j * HD:(j + 1) * HD], BKt[:, j, c, p * HD:(p + 1) * HD],
                                      SV[:, j, c, p * HD:(p + 1) * HD], start=True, stop=True)
                    return last

                def gn_mean(_):
                    pe.wait_ge(dve_done["chunk_z"], CHUNKS)
                    pe.wait_ge(act_done["chunk_o"], CHUNKS)
                    return tiles(4, lambda j: blk, lambda j: OT[:, j, :])

                def gn_var(_):
                    pe.wait_ge(dve_done["gn_mean"], 1)
                    pe.wait_ge(pool_done["gn_sq"], 1)
                    return head_sums(4, OSQ)

                def gn_T(_):
                    pe.wait_ge(dve_done["gn_var"], 1)
                    pe.wait_ge(pool_done["gn_pow"], 1)
                    return rows_of_heads(4, R8b)

                def gn_scale(_):
                    pe.wait_ge(dve_done["gn_T"], 1)
                    return tiles(4, lambda j: selT8[0:HEADS, j, :], lambda j: R8bT)

                def heads_T(src, b, n=PAIRS):
                    for j in range(n):
                        for m in range(TT):
                            last = nc.tensor.transpose(pair_tiles(b)[:, j, m * P:(m + 1) * P],
                                                       src[:, m, j * P:(j + 1) * P], ident)
                    return last

                def trq(b):
                    if b == 1:
                        pe.wait_ge(dve_done["merge_u"], LEVELS)
                    else:
                        pe.wait_ge(dve_done["oT"], 2)
                    pe.wait_ge(dve_done["rope"], {1: 2, 2: 4}[b])
                    return heads_T(QTOK, 6)

                def trk(b):
                    pe.wait_ge(act_done["trq"], b)
                    pe.wait_ge(dve_done["rope"], {1: 3, 2: 4}[b])
                    return heads_T(KTOK, 6) if b == 1 else heads_T(SKTOK, 6, 2)

                def key_of(b, h, m0, m1):
                    rows = slice(64 * (h % 2), 64 * (h % 2) + 64)
                    return KTt[rows, h // 2 if b == 1 else h // 4, m0 * P:m1 * P]

                def scores(b, pair):
                    if pair:
                        pe.wait_ge(dve_done["pv"], 4 * (b - 1) + pair)
                    if pair == 0:
                        pe.wait_ge(act_done["trk"], b)
                    for h in (2 * pair, 2 * pair + 1):
                        q = QT[64 * (h % 2):64 * (h % 2) + 64, pair, :]
                        mm(psum[:, 6 + h % 2, 0:P], q[:, 0:P], key_of(b, h, 0, 1), start=True, stop=True)
                        last = mm(psum[:, 6 + h % 2, P:3 * P], q[:, P:2 * P], key_of(b, h, 0, 2), start=True, stop=True)
                    return last

                def pT(b, pair):
                    pe.wait_ge(act_done["exps"], 4 * (b - 1) + pair + 1)
                    for h in range(2):
                        for i in range(3):
                            last = nc.tensor.transpose(psum[:, 6 + h, i * P:(i + 1) * P], probs[:, h, i * P:(i + 1) * P],
                                                       ident)
                    return last

                def pv(b, pair):
                    if b == 1 and pair == 0:
                        pe.wait_ge(*taken("mv"))
                    pe.wait_ge(dve_done["pT"], 4 * (b - 1) + pair + 1)
                    for m in range(TT):
                        for h in range(2):
                            g = 2 * pair + h
                            dst = psum[:, 6, (2 * m + h) * HD:(2 * m + h + 1) * HD]
                            for k in range(m + 1):
                                v = VTOK[:, k, g * HD:(g + 1) * HD] if b == 1 else \
                                    SVTOK[:, k, (g // 4) * HD:(g // 4 + 1) * HD]
                                at = (m + k) * P
                                last = mm(dst, probsT[:, h, at:at + P], v, start=(k == 0), stop=(k == m))
                    return last

                def oT_(b):
                    pe.wait_ge(dve_done["pv"], 4 * b)
                    return heads_T(QTOK, 6)

                def yT(_):
                    pe.wait_ge(dve_done["mem_T"], 1)
                    pe.wait_ge(*taken("branch01"))
                    return to_features(ACC)

                def xscores(h):
                    if h < 2:
                        pe.wait_ge(dve_done["pre_T"], 2 * KT)
                    else:
                        pe.wait_ge(dve_done["xpv"], h - 1)
                    if h == 0:
                        pe.wait_ge(*taken("xq"))
                    for m in range(TT):
                        last = mm(psum[:, 4 + h % 2, m * MEM:(m + 1) * MEM], XQT[:, h, m * P:(m + 1) * P], xkT[:, h, :],
                                  start=True, stop=True)
                    return last

                def xpT(h):
                    if h >= 2:
                        pe.wait_ge(dve_done["xpT"], h - 1)
                    pe.wait_ge(act_done["xscores"], h + 1)
                    for k in range(TT):
                        for m in range(TT):
                            at = k * SEQ + m * P
                            last = nc.tensor.transpose(psum[:, 6 + h % 2, at:at + P], XP[:, h % 2, m, k * P:(k + 1) * P],
                                                       ident)
                    return last

                def xpv(h):
                    pe.wait_ge(dve_done["xpT"], h + 1)
                    for m in range(TT):
                        for k in range(TT):
                            last = mm(psum[:, 4 + h % 2, m * XD:(m + 1) * XD], XPT[:, h % 2, k, m * P:(m + 1) * P],
                                      xv[:, k, h * XD:(h + 1) * XD], start=(k == 0), stop=(k == TT - 1))
                    return last

                def xoT(_):
                    pe.wait_ge(dve_done["xpv"], XH)
                    return heads_T(XO, 6)

                def hiddenT(h):
                    if h < 2:
                        pe.wait_ge(dve_done["pre_T"], 3 * KT)
                    else:
                        pe.wait_ge(act_done["hiddenT"], h - 1)
                    pe.wait_ge(*taken(f"up{h}"))
                    return heads_T(RELU[:, h % 2], 4 + 2 * (h % 2))

                parts = {"params": params, "pre_T": pre_T, "vres_down": vres_down, "lora_up": lora_up_,
                         "lora_g": lora_g, "kk_sum": kk_sum, "kk_T": kk_T, "kk_scale": kk_scale, "vres_up": vres_up,
                         "bonus": bonus, "v_token": v_token, "bk_token": bk_token, "low": low,
                         "merge_p": merge_p, "merge_u": merge_u, "merge_l": merge_l, "chunk_m": chunk_m, "chunk_x": chunk_x,
                         "chunk_sa": chunk_sa, "chunk_o": chunk_o, "chunk_z": chunk_z, "gn_mean": gn_mean,
                         "gn_var": gn_var, "gn_T": gn_T, "gn_scale": gn_scale, "trq": trq, "trk": trk, "scores": scores,
                         "pT": pT, "pv": pv, "oT": oT_, "yT": yT, "xscores": xscores, "xpT": xpT, "xpv": xpv,
                         "xoT": xoT, "hiddenT": hiddenT, "mem_T": mem_T}
                for kind, *which in ORDER:
                    if kind == "gemm":
                        gemm(*which)
                    elif kind in parts:
                        parts[kind](*which).then_inc(pe_done[kind], 1)
                pe.drain().then_inc(layer_end, 1)
                pe.wait_ge(layer_clear, l + 1)

        @block.scalar
        def _(act):
            A = nc.scalar.activation

            for m in range(TT):
                act.dma_start(pos[:, m:m + 1], t["positions"][0, m * P:(m + 1) * P].rearrange("(p a) -> p a", a=1)) \
                    .then_inc(start_pos, 16)
            act.dma_start(cst[:, INVF_AT:NCONST], t["consts"][:, INVF_AT:NCONST]).then_inc(start_invf, 16)
            for dst, src, loaded in parameters(0):
                act.dma_start(dst, src).then_inc(loaded, 16)
            act.wait_ge(angles_ready, 1)
            A(sin[:, :, :], angle, ACT.Sin)
            A(cos[:, :, :], angle, ACT.Sin, scale=0.5).then_inc(sines_ready, 1)
            act.wait_ge(start_x, 16)

            with act.Fori(0, DEPTH) as l:
                count = Counts()

                def pre_scale(n):
                    if n:
                        act.wait_ge(dve_done["post"], n)
                    for m in range(TT):
                        last = A(SQ[:, m * D:(m + 1) * D], x[:, m, :], ACT.Square, accum_out=stat[:, m:m + 1])
                    last.then_inc(act_done["squares"], 1)
                    act.wait_ge(act_done["squares"], count("squares"))

                def take(name):
                    b0 = BANK0[name]
                    act.wait_ge(weights_used, after(l, name))
                    two = psum[:, b0:b0 + 2, :]
                    if name == "xk":
                        last = A(xkT[:, :, :].rearrange("p h s -> p (h s)"), two, ACT.Copy)
                    elif name == "xv":
                        last = A(xv[:, :, :], two, ACT.Copy)
                    elif name == "lora":
                        act.wait_ge(pool_done["zero"], 1)
                        last = A(U2[:, :, 1:SEQ + 1], bank(b0).rearrange("p (f s) -> p f s", s=SEQ), ACT.Copy)
                    elif name in ("k", "v", "r"):
                        if name != "k":
                            act.wait_ge(dve_done["lerp"], {"v": 1, "r": 2}[name])
                        last = A(U[:, :, 1:SEQ + 1], pair_tiles(b0), ACT.Copy)
                    elif name == "mv":
                        last = A(VTOK, two, ACT.Copy)
                    elif name[:4] == "gate":
                        if name[4] != "1":
                            act.wait_ge(*taken({"2": "branch1", "0": "branch2"}[name[4]] + name[5]))
                        last = A(gates[:, int(name[5]), :, :], two, ACT.Tanh, scale=0.5)
                    elif name == "xq":
                        last = A(XQT.rearrange("p h s -> p (h s)"), two, ACT.Copy)
                    last.then_inc(act_done["gemm"], 1)
                    act.wait_ge(act_done["gemm"], count("gemm"))

                def split_high(u):
                    act.wait_ge(weights_loaded[u % RING], l * (16 * slot_loads(u)) + 16 * (u // RING + 1))
                    act.wait_ge(weights_used, l * NW + (RING + u - HIGH + 1))
                    A(high[:, u % HIGH, :], ring[:, u % RING, :], ACT.Copy).then_inc(act_done["split_high"], 1)

                def pre_T(n):
                    act.wait_ge(pe_done["pre_T"], n + 1)
                    gain = ("mix_pre", "xattn_pre", "mlp_pre")[n]
                    for k in range(KT):
                        A(hT[:, k, :], psum[:, 4 + k // 2, (k % 2) * SEQ:(k % 2 + 1) * SEQ], ACT.Copy,
                          scale=pc(gain, k)).then_inc(act_done["pre_T"], 1)

                def mem_squares(_):
                    act.wait_ge(mem_in, (l + 1) * 16)
                    for m in range(TT):
                        last = A(SQ[:, m * D:(m + 1) * D], mem_rows[:, m, :], ACT.Square, accum_out=stat[:, 12 + m:13 + m])
                    last.then_inc(act_done["mem_squares"], 1)
                    act.wait_ge(act_done["mem_squares"], count("mem_squares"))

                def mem_T(_):
                    act.wait_ge(pe_done["mem_T"], 1)
                    for k in range(KT):
                        A(mT_high[:, k, :], psum[:, 4 + k // 2, (k % 2) * MEM:(k % 2 + 1) * MEM], ACT.Copy,
                          scale=pc("mem", k)).then_inc(act_done["mem_T"], 1)

                def v_down_split(_):
                    act.wait_ge(loras_in, (l + 1) * (16 * N_LORAS))
                    A(v_down_high[:, :, :], v_down[:, :, :], ACT.Copy).then_inc(act_done["v_down"], 1)

                def rw_high(_):
                    act.wait_ge(dve_done["rw_o"], 1)
                    A(RWO_high, RWO, ACT.Copy).then_inc(act_done["rw_high"], 1)

                def lora_tanh(_):
                    act.wait_ge(dve_done["lora_lerp"], 1)
                    A(TWA[0:64, :], TWA[0:64, :], ACT.Tanh)
                    A(SG, SG, ACT.Tanh, scale=0.5).then_inc(act_done["lora_tanh"], 1)
                    act.wait_ge(act_done["lora_tanh"], count("lora_tanh"))

                def vres_down(_):
                    act.wait_ge(pe_done["vres_down"], 1)
                    A(UV[:, 1:SEQ + 1], psum[0:32, 4, 0:SEQ], ACT.Copy).then_inc(act_done["vres_down"], 1)
                    act.wait_ge(act_done["vres_down"], count("vres_down"))

                def lora_up_(_):
                    act.wait_ge(pe_done["lora_up"], 1)
                    for j in range(PAIRS):
                        A(A1[:, j, :], pair_tiles(6)[:, j, :], ACT.Tanh, scale=0.5, bias=half[:, j:j + 1])
                        last = A(TA[:, j, :], pair_tiles(4)[:, j, :], ACT.Tanh, scale=0.5, bias=half[:, 4 + j:5 + j])
                    last.then_inc(act_done["lora_up"], 1)
                    act.wait_ge(act_done["lora_up"], count("lora_up"))

                def lora_g(_):
                    act.wait_ge(pe_done["lora_g"], 1)
                    A(G.rearrange("p j s -> p (j s)"), psum[:, 4:6, :], ACT.Copy).then_inc(act_done["lora_g"], 1)
                    act.wait_ge(act_done["lora_g"], count("lora_g"))

                def decay(_):
                    act.wait_ge(dve_done["scan"], 1)
                    A(A3, A2, ACT.Exp, scale=-LOGW).then_inc(act_link, 1)
                    act.wait_ge(act_link, count("link"))
                    A(A1, A1, ACT.Exp, scale=LOGW)
                    A(A2, A2, ACT.Exp, scale=LOGW).then_inc(act_done["decay"], 1)
                    act.wait_ge(act_done["decay"], count("decay"))

                def vres_up(_):
                    act.wait_ge(pe_done["vres_up"], 1)
                    for j in range(PAIRS):
                        last = A(VG[:, j, :], pair_tiles(6)[:, j, :], ACT.Tanh, scale=0.5, bias=half[:, 8 + j:9 + j])
                    last.then_inc(act_done["vres_up"], 1)
                    act.wait_ge(act_done["vres_up"], count("vres_up"))

                def v_token(_):
                    act.wait_ge(pe_done["v_token"], 1)
                    A(SV[64:128, :, :, :].rearrange("p j c t -> p (j c t)"), psum[64:128, 4:8, :], ACT.Copy) \
                        .then_inc(act_done["v_token"], 1)
                    act.wait_ge(act_done["v_token"], count("v_token"))

                def bk_token(_):
                    act.wait_ge(pe_done["bk_token"], 1)
                    A(BKt.rearrange("p j c t -> p (j c t)"), psum[:, 4:8, :], ACT.Copy) \
                        .then_inc(act_done["bk_token"], 1)
                    act.wait_ge(act_done["bk_token"], count("bk_token"))

                def by_parity(dst, b, kind):
                    for p in range(2):
                        last = A(dst[:, p::2, :, :].rearrange("p j c t -> p j (c t)"),
                                 bank(b + p).rearrange("p (j t) -> p j t", j=PAIRS), ACT.Copy)
                    last.then_inc(act_done[kind], 1)
                    act.wait_ge(act_done[kind], count(kind))

                def low(_):
                    act.wait_ge(pe_done["low"], 1)
                    act.wait_ge(pool_done["zero"], 2)
                    act.wait_ge(dve_done["bonus"], 1)
                    by_parity(Nl, 4, "low")

                def merge_p(n):
                    act.wait_ge(pe_done["merge_p"], n + 1)
                    by_parity(P1, 4, "merge_p")

                def chunk_x(c):
                    act.wait_ge(pe_done["chunk_x"], c + 1)
                    rows = slice(64 * (c % 2), 64 * (c % 2) + 64)
                    A(XS[rows, :], psum[rows, 4, :], ACT.Copy).then_inc(act_done["chunk_x"], 1)
                    act.wait_ge(act_done["chunk_x"], count("chunk_x"))

                def chunk_sa(c):
                    act.wait_ge(pe_done["chunk_sa"], c + 1)
                    A(SV[0:64, :, c, :], psum[0:64, 5, :].rearrange("p (j t) -> p j t", j=PAIRS), ACT.Copy) \
                        .then_inc(act_done["chunk_sa"], 1)
                    act.wait_ge(act_done["chunk_sa"], count("chunk_sa"))

                def chunk_o(c):
                    act.wait_ge(pe_done["chunk_o"], c + 1)
                    A(OT[:, :, c * CHUNK:(c + 1) * CHUNK],
                      psum[:, 4, 0:PAIRS * CHUNK].rearrange("p (j t) -> p j t", j=PAIRS), ACT.Copy) \
                        .then_inc(act_done["chunk_o"], 1)
                    act.wait_ge(act_done["chunk_o"], count("chunk_o"))

                def trq(b):
                    act.wait_ge(pe_done["trq"], b)
                    A(QT.rearrange("p j s -> p (j s)"), psum[:, 6:8, :], ACT.Copy).then_inc(act_done["trq"], 1)
                    act.wait_ge(act_done["trq"], count("trq"))

                def trk(b):
                    act.wait_ge(pe_done["trk"], b)
                    n = PAIRS if b == 1 else 2
                    A(KTt[:, 0:n, :], pair_tiles(6)[:, 0:n, :], ACT.Copy).then_inc(act_done["trk"], 1)
                    act.wait_ge(act_done["trk"], count("trk"))

                def exps(b, pair):
                    n = 4 * (b - 1) + pair
                    act.wait_ge(dve_done["scores"], n + 1)
                    s0 = 20 * (n % 2)
                    for h in range(2):
                        for m in range(TT):
                            i = 2 * h + m
                            cols = slice(0, P) if m == 0 else slice(P, 3 * P)
                            last = A(probs[:, h, cols], probs[:, h, cols], ACT.Exp, scale=HD ** -0.5,
                                     bias=soft[:, s0 + i:s0 + i + 1], accum_out=soft[:, s0 + 4 + i:s0 + 5 + i])
                    if b == 2:
                        last = A(soft[:, s0 + 16:s0 + 20], soft[:, s0 + 16:s0 + 20], ACT.Exp)
                    last.then_inc(act_done["exps"], 1)
                    act.wait_ge(act_done["exps"], count("exps"))

                def high_parts(stage, high_part, b0, banks, scale=1.0):
                    for b in range(banks):
                        A(high_part[:, 2 * b:2 * b + 2, :], bank(b0 + b).rearrange("p (k s) -> p k s", s=SEQ), ACT.Copy,
                          scale=scale).then_inc(act_done[stage], 1)
                        act.wait_ge(act_done[stage], count(stage))

                def oT_(b):
                    act.wait_ge(pe_done["oT"], b)
                    high_parts("oT", oT, 6, 2)

                def yT(_):
                    act.wait_ge(pe_done["yT"], 1)
                    high_parts("yT", YT, 4, 4, 0.5)

                def post_squares(name, h):
                    act.wait_ge(weights_used, after(l, name))
                    for m in range(TT):
                        b = 2 * h + m if name == "down" else BANK0[name] + m
                        A(SQ[:, (2 * h + m) * COLS:(2 * h + m + 1) * COLS], bank(b), ACT.Square,
                          accum_out=stat[:, 8 + 2 * m + h:9 + 2 * m + h]).then_inc(act_done["post_squares"], 1)
                        act.wait_ge(act_done["post_squares"], count("post_squares"))

                def xscores(h):
                    act.wait_ge(pe_done["xscores"], h + 1)
                    act.wait_ge(dve_done["xmax"], h + 1)
                    s0 = 20 * (h % 2)
                    for m in range(TT):
                        last = A(XP[:, h % 2, m, :], psum[:, 4 + h % 2, m * MEM:(m + 1) * MEM], ACT.Exp,
                                 scale=stat[:, 6 + m:7 + m], bias=soft[:, s0 + m:s0 + m + 1],
                                 accum_out=soft[:, s0 + 4 + m:s0 + 5 + m])
                    last.then_inc(act_done["xscores"], 1)
                    act.wait_ge(act_done["xscores"], count("xscores"))

                def xoT(_):
                    act.wait_ge(pe_done["xoT"], 1)
                    high_parts("xoT", XOT, 6, 2)

                def hiddenT(h):
                    act.wait_ge(pe_done["hiddenT"], h + 1)
                    b = 4 + 2 * (h % 2)
                    if h:
                        act.wait_ge(dve_done["hiddenT"], h)
                    A(SQUARED.rearrange("p j s -> p (j s)"), psum[:, b:b + 2, :], ACT.Square).then_inc(act_link, 1)
                    act.wait_ge(act_link, count("link"))
                    A(HID[:, 4 * h:4 * h + 4, :], SQUARED, ACT.Copy).then_inc(act_done["hiddenT"], 1)
                    act.wait_ge(act_done["hiddenT"], count("hiddenT"))

                parts = {"pre_scale": pre_scale, "lora_tanh": lora_tanh, "vres_down": vres_down,
                         "lora_up": lora_up_, "lora_g": lora_g, "decay": decay, "vres_up": vres_up,
                         "v_token": v_token, "bk_token": bk_token, "low": low, "merge_p": merge_p,
                         "chunk_x": chunk_x, "chunk_sa": chunk_sa, "chunk_o": chunk_o, "trq": trq, "trk": trk,
                         "scores": exps, "oT": oT_, "yT": yT, "xscores": xscores, "xoT": xoT, "hiddenT": hiddenT,
                         "split_high": split_high, "pre_T": pre_T, "mem_scale": mem_squares, "mem_T": mem_T, "v_down": v_down_split, "rw_high": rw_high}
                for kind, *which in ORDER:
                    if kind == "gemm":
                        name, q = which
                        if q == pieces(name) - 1:
                            if TAKER[name] == "act":
                                take(name)
                            for h in POST_HALVES.get(name, ()):
                                post_squares(name, h)
                    elif kind in parts:
                        parts[kind](*which)
                        if (kind, *which) == ("chunk_o", CHUNKS - 1):
                            act.dma_start(mem_rows, t["mem"][0].rearrange("(t p) n -> p t n", p=P)) \
                                .then_inc(mem_in, 16)
                act.drain().then_inc(layer_end, 1)
                act.wait_ge(layer_clear, l + 1)

        @block.vector
        def _(dve):
            v = nc.vector
            start_count = Counts()
            v.memset(not_first[:, :], 0.0)
            dve.wait_ge(pool_start, 1)
            dve.wait_ge(start_pos, 16 * TT)
            dve.wait_ge(start_invf, 16)
            v.tensor_copy(pos_f, pos[:, :]).then_inc(start_link, 1)
            dve.wait_ge(start_link, start_count("link"))
            for m in range(TT):
                last = v.tensor_scalar(angle[:, m, :], invf, pos_f[:, m:m + 1], None, ALU.mult)
            last.then_inc(start_link, 1)
            dve.wait_ge(start_link, start_count("link"))
            v.tensor_scalar(turns, angle, 1 / (2 * math.pi), ROUND, ALU.mult, ALU.add).then_inc(start_link, 1)
            dve.wait_ge(start_link, start_count("link"))
            v.tensor_scalar(turns, turns, ROUND, None, ALU.subtract).then_inc(start_link, 1)
            dve.wait_ge(start_link, start_count("link"))
            for part in TWO_PI_PARTS:
                v.scalar_tensor_tensor(angle, turns, -part, angle, ALU.mult, ALU.add).then_inc(start_link, 1)
                dve.wait_ge(start_link, start_count("link"))
            v.tensor_scalar(angle, angle, 3.1415925, -3.1415925, ALU.min, ALU.max).then_inc(angles_ready, 1)
            dve.wait_ge(sines_ready, 1)
            v.tensor_tensor(cos[:, :, :], cos[:, :, :], cos[:, :, :], ALU.mult).then_inc(start_link, 1)
            dve.wait_ge(start_link, start_count("link"))
            v.tensor_scalar(cos[:, :, :], cos[:, :, :], -2.0, 1.0, ALU.mult, ALU.add).then_inc(start_link, 1)
            dve.wait_ge(start_link, start_count("link"))

            with dve.Fori(0, DEPTH) as l:
                count = Counts()

                def rotate(src, dst, m, heads, scratch, copies=1):
                    s = src.rearrange("p (h d) -> p h d", d=HD)
                    a, b = s[:, :, 0:HD // 2], s[:, :, HD // 2:HD]
                    c = cos[:, m, :].unsqueeze(1).broadcast_to([P, heads, HD // 2])
                    sn = sin[:, m, :].unsqueeze(1).broadcast_to([P, heads, HD // 2])
                    w = [scratch[:, i * heads * 32:(i + 1) * heads * 32].rearrange("p (h d) -> p h d", d=HD // 2)
                         for i in range(4)]
                    v.tensor_tensor(w[0], a, c, ALU.mult)
                    v.tensor_tensor(w[1], b, sn, ALU.mult)
                    v.tensor_tensor(w[2], b, c, ALU.mult)
                    v.tensor_tensor(w[3], a, sn, ALU.mult).then_inc(dve_link, 1)
                    dve.wait_ge(dve_link, count("link"))
                    d = dst.rearrange("p (h e d) -> p h e d", e=copies, d=HD)
                    for e in range(copies):
                        v.tensor_tensor(d[:, :, e, 0:HD // 2], w[0], w[1], ALU.subtract)
                        last = v.tensor_tensor(d[:, :, e, HD // 2:HD], w[2], w[3], ALU.add)
                    return last

                def lerp(dst, mu):
                    v.tensor_tensor(TMP, U[:, :, 0:SEQ], U[:, :, 1:SEQ + 1], ALU.subtract).then_inc(dve_link, 1)
                    dve.wait_ge(dve_link, count("link"))
                    for j in range(PAIRS):
                        last = v.scalar_tensor_tensor(dst[:, j, :], TMP[:, j, :], pc("mu", mu + j),
                                                      U[:, j, 1:SEQ + 1], ALU.mult, ALU.add)
                    last.then_inc(dve_done["lerp"], 1)
                    dve.wait_ge(dve_done["lerp"], count("lerp"))

                def per_pair(dst, src, scale, add=None):
                    for j in range(PAIRS):
                        last = v.tensor_scalar(dst[:, j, :], src[:, j, :], scale(j), add and add(j), ALU.mult,
                                               ALU.add if add else ALU.bypass)
                    return last

                def take(name):
                    b0 = BANK0[name]
                    dve.wait_ge(weights_used, after(l, name))
                    gemm_done = dve_done["gemm"]
                    if name == "skv":
                        for m in range(TT):
                            src = psum[:, b0, m * 256:(m + 1) * 256]
                            if m:
                                last.then_inc(dve_link, 1)
                                dve.wait_ge(dve_link, count("link"))
                            last = rotate(src[:, 0:P], SKTOK[:, m, :], m, 2, LTMP, copies=2)
                        last.then_inc(dve_done["rope"], 1)
                        dve.wait_ge(dve_done["rope"], count("rope"))
                        v.tensor_copy(SVTOK, bank(b0).rearrange("p (m c) -> p m c", m=TT)[:, :, P:2 * P]) \
                            .then_inc(gemm_done, 1)
                        dve.wait_ge(dve_done["gemm"], count("gemm"))
                    elif name in ("mq", "mk", "sq"):
                        dst = KTOK if name == "mk" else QTOK
                        for m in range(TT):
                            if m:
                                last.then_inc(dve_link, 1)
                                dve.wait_ge(dve_link, count("link"))
                            last = rotate(bank(b0 + m), dst[:, m, :], m, HEADS, RSCR)
                        last.then_inc(dve_done["rope"], 1)
                        dve.wait_ge(dve_done["rope"], count("rope"))
                        v.tensor_copy(soft[:, 39:40], neg_half[:, 0:1]).then_inc(gemm_done, 1)
                        dve.wait_ge(dve_done["gemm"], count("gemm"))
                    elif name[:6] == "branch":
                        h = int(name[7])
                        cols = slice(h * COLS, (h + 1) * COLS)
                        dve.wait_ge(*taken(f"gate{name[6]}{h}"))
                        two = psum[:, b0:b0 + 2, :]
                        if name[6] == "1":
                            v.scalar_tensor_tensor(ACC[:, :, cols], gates[:, h, :, :], 1.0, two, ALU.add, ALU.mult) \
                                .then_inc(gemm_done, 1)
                            dve.wait_ge(dve_done["gemm"], count("gemm"))
                        else:
                            v.scalar_tensor_tensor(gates[:, h, :, :], gates[:, h, :, :], 1.0, two, ALU.add,
                                                   ALU.mult).then_inc(dve_link, 1)
                            dve.wait_ge(dve_link, count("link"))
                            v.tensor_tensor(ACC[:, :, cols], ACC[:, :, cols], gates[:, h, :, :], ALU.add) \
                                .then_inc(gemm_done, 1)
                            dve.wait_ge(dve_done["gemm"], count("gemm"))
                    elif name[:2] == "up":
                        dve.wait_ge(pool_done["rstd"], 3)
                        for m in range(TT):
                            last = v.tensor_scalar(RELU[:, int(name[2]) % 2, m, :], bank(b0 + m), stat[:, 4 + m:5 + m],
                                                   0.0, ALU.mult, ALU.max)
                        last.then_inc(gemm_done, 1)
                        dve.wait_ge(dve_done["gemm"], count("gemm"))

                def times_gain(name, h):
                    n = {"out": 1, "xo": 2, "down": 3}[name.rstrip("01")]
                    dve.wait_ge(post_gain_in, l * 48 + 16 * n)
                    cols = slice(h * COLS, (h + 1) * COLS)
                    for m in range(TT):
                        b = 2 * h + m if name == "down" else BANK0[name] + m
                        dve.wait_ge(act_done["post_squares"], 4 * (n - 1) + 2 * h + m + 1)
                        last = v.tensor_tensor(POST[:, m, cols], bank(b), post_gain[:, cols], ALU.mult)
                    last.then_inc(dve_done["gemm"], 1)
                    dve.wait_ge(dve_done["gemm"], count("gemm"))

                def post(n):
                    dve.wait_ge(pool_done["post_rstd"], n)
                    for m in range(TT):
                        last = v.scalar_tensor_tensor(x[:, m, :], POST[:, m, :], stat[:, 20 + m:21 + m], x[:, m, :],
                                                      ALU.mult, ALU.add)
                    last.then_inc(dve_done["post"], 1)
                    dve.wait_ge(dve_done["post"], count("post"))

                def params(_):
                    dve.wait_ge(pe_done["params"], 1)
                    v.tensor_copy(pcol[:, :], psum[:, 4, 0:NPROW]).then_inc(dve_link, 1)
                    dve.wait_ge(dve_link, count("link"))
                    for i, name in enumerate(("w0", "a0", "v0", "k_a")):
                        v.tensor_scalar(half[:, 4 * i:4 * i + 4], pc(name, 0, 4), 0.5, None, ALU.mult)
                    v.tensor_scalar(half[:, 16:20], pc("k_a", 0, 4), -0.5, 1.0, ALU.mult, ALU.add) \
                        .then_inc(dve_done["params"], 1)
                    dve.wait_ge(dve_done["params"], count("params"))

                def split_low(u):
                    dve.wait_ge(act_done["split_high"], u + 1)
                    v.tensor_tensor(ring_low[:, u % RING, :], ring[:, u % RING, :], high[:, u % HIGH, :].bitcast(F32), ALU.subtract) \
                        .then_inc(dve_done["split_low"], 1)

                def low_part(stage, low, value, high_part):
                    v.tensor_tensor(low, value, high_part.bitcast(F32), ALU.subtract).then_inc(dve_done[stage], 1)
                    dve.wait_ge(dve_done[stage], count(stage))

                def low_parts(stage, low, high_part, b0, banks, before, scale=1.0):
                    for b in range(banks):
                        dve.wait_ge(act_done[stage], before + b + 1)
                        v.scalar_tensor_tensor(low[:, 2 * b:2 * b + 2, :], bank(b0 + b).rearrange("p (k s) -> p k s", s=SEQ),
                                               scale, high_part[:, 2 * b:2 * b + 2, :].bitcast(F32), ALU.mult,
                                               ALU.subtract).then_inc(dve_done[stage], 1)
                        dve.wait_ge(dve_done[stage], count(stage))

                def v_down_split(_):
                    dve.wait_ge(act_done["v_down"], 1)
                    low_part("v_down", v_down_low[:, :, :], v_down[:, :, :], v_down_high[:, :, :])

                def mem_scale(_):
                    dve.wait_ge(pool_done["mem_rstd"], 1)
                    for m in range(TT):
                        last = v.tensor_scalar(mem_rows[:, m, :], mem_rows[:, m, :], stat[:, 14 + m:15 + m], None, ALU.mult)
                    last.then_inc(dve_done["mem_scale"], 1)
                    dve.wait_ge(dve_done["mem_scale"], count("mem_scale"))

                def mem_T(_):
                    for k in range(KT):
                        dve.wait_ge(act_done["mem_T"], 2 * (k // 2) + 2)
                        last = v.scalar_tensor_tensor(mT_low[:, k, :],
                                                      psum[:, 4 + k // 2, (k % 2) * MEM:(k % 2 + 1) * MEM], pc("mem", k),
                                                      mT_high[:, k, :].bitcast(F32), ALU.mult, ALU.subtract)
                    last.then_inc(dve_done["mem_T"], 1)
                    dve.wait_ge(dve_done["mem_T"], count("mem_T"))

                def rw_low(_):
                    dve.wait_ge(act_done["rw_high"], 1)
                    low_part("rw_low", RWO_low, RWO, RWO_high)

                def oT_(b):
                    low_parts("oT", oT_low, oT, 6, 2, 2 * (b - 1))

                def yT(_):
                    low_parts("yT", YT_low, YT, 4, 4, 0, 0.5)

                def xoT(_):
                    low_parts("xoT", XOT_low, XOT, 6, 2, 0)

                def hiddenT(h):
                    dve.wait_ge(act_done["hiddenT"], h + 1)
                    low_part("hiddenT", HID_low[:, 4 * h:4 * h + 4, :], SQUARED, HID[:, 4 * h:4 * h + 4, :])

                def pre_scale(n):
                    if n:
                        return
                    dve.wait_ge(pool_done["rstd"], 1)
                    for m in range(TT):
                        last = v.tensor_scalar(hrow[:, m, :], x[:, m, :], stat[:, 4 + m:5 + m], None, ALU.mult)
                    last.then_inc(dve_done["pre_scale"], 1)
                    dve.wait_ge(dve_done["pre_scale"], count("pre_scale"))

                def pre_T(n):
                    gain = ("mix_pre", "xattn_pre", "mlp_pre")[n]
                    for k in range(KT):
                        dve.wait_ge(act_done["pre_T"], n * KT + 2 * (k // 2) + 2)
                        v.scalar_tensor_tensor(hT_low[:, k, :], psum[:, 4 + k // 2, (k % 2) * SEQ:(k % 2 + 1) * SEQ],
                                               pc(gain, k), hT[:, k, :].bitcast(F32), ALU.mult, ALU.subtract) \
                            .then_inc(dve_done["pre_T"], 1)
                    dve.wait_ge(dve_done["pre_T"], (n + 1) * KT)

                def lora_lerp(_):
                    dve.wait_ge(*taken("lora"))
                    v.tensor_tensor(XS2, U2[:, :, 0:SEQ], U2[:, :, 1:SEQ + 1], ALU.subtract).then_inc(dve_link, 1)
                    dve.wait_ge(dve_link, count("link"))
                    v.scalar_tensor_tensor(TWA, XS2[:, 0, :], pc("mu", 12), U2[:, 0, 1:SEQ + 1], ALU.mult, ALU.add)
                    v.scalar_tensor_tensor(SG, XS2[:, 1, :], pc("mu", 13), U2[:, 1, 1:SEQ + 1], ALU.mult, ALU.add) \
                        .then_inc(dve_done["lora_lerp"], 1)
                    dve.wait_ge(dve_done["lora_lerp"], count("lora_lerp"))

                def lora_sig(_):
                    dve.wait_ge(act_done["lora_tanh"], 1)
                    v.tensor_scalar(SG, SG, 0.5, 0.5, ALU.mult, ALU.add).then_inc(dve_done["lora_sig"], 1)
                    dve.wait_ge(dve_done["lora_sig"], count("lora_sig"))

                def vres_lerp(_):
                    dve.wait_ge(act_done["vres_down"], 1)
                    v.tensor_tensor(LTMP[0:32, :], UV[:, 0:SEQ], UV[:, 1:SEQ + 1], ALU.subtract) \
                        .then_inc(dve_link, 1)
                    dve.wait_ge(dve_link, count("link"))
                    dve.wait_ge(loras_in, (l + 1) * (16 * N_LORAS))
                    v.scalar_tensor_tensor(VM[0:32, :], LTMP[0:32, :], v_mu[:, 0:1], UV[:, 1:SEQ + 1], ALU.mult,
                                           ALU.add).then_inc(dve_done["vres_lerp"], 1)
                    dve.wait_ge(dve_done["vres_lerp"], count("vres_lerp"))

                def scan(_):
                    dve.wait_ge(act_done["lora_up"], 1)
                    v.tensor_scalar(A1, A1, 1.0, None, ALU.add).then_inc(dve_link, 1)
                    dve.wait_ge(dve_link, count("link"))
                    for j in range(PAIRS):
                        last = v.tensor_tensor_scan(A2[:, j, :], RESET, A1[:, j, :], 0.0, ALU.mult, ALU.add)
                    last.then_inc(dve_link, 1)
                    dve.wait_ge(dve_link, count("link"))
                    v.tensor_tensor(A1, A2, A1, ALU.subtract).then_inc(dve_done["scan"], 1)
                    dve.wait_ge(dve_done["scan"], count("scan"))

                def k_in(_):
                    dve.wait_ge(*taken("k"))
                    lerp(Ks, 4)
                    per_pair(KK, Ks, lambda j: pc("k_k", j)).then_inc(dve_done["kk"], 1)
                    dve.wait_ge(dve_done["kk"], count("kk"))

                def kk_sum(_):
                    dve.wait_ge(pe_done["kk_sum"], 1)
                    v.tensor_scalar(S8, psum[:, 6, 0:TT * HEADS], 1e-24, None, ALU.max) \
                        .then_inc(dve_done["kk_sum"], 1)
                    dve.wait_ge(dve_done["kk_sum"], count("kk_sum"))

                def kk_T(_):
                    dve.wait_ge(pe_done["kk_T"], 1)
                    v.tensor_copy(R8T, psum[0:HEADS, 6, 0:SEQ]).then_inc(dve_done["kk_T"], 1)
                    dve.wait_ge(dve_done["kk_T"], count("kk_T"))

                def kk_scale(_):
                    dve.wait_ge(pe_done["kk_scale"], 1)
                    v.tensor_tensor(KK, KK, pair_tiles(4), ALU.mult).then_inc(dve_done["kk_scale"], 1)
                    dve.wait_ge(dve_done["kk_scale"], count("kk_scale"))

                def v_in(_):
                    dve.wait_ge(*taken("v"))
                    lerp(V, 8)

                def flat(a):
                    return a.rearrange("p j (c t) -> p (j c) t", t=CHUNK)

                def fold_k(_):
                    dve.wait_ge(act_done["decay"], 1)
                    per_pair(TMP, TA, lambda j: half[:, 12 + j:13 + j], lambda j: half[:, 16 + j:17 + j]) \
                        .then_inc(dve_link, 1)
                    dve.wait_ge(dve_link, count("link"))
                    v.tensor_tensor(Ks, Ks, TMP, ALU.mult).then_inc(dve_link, 1)
                    dve.wait_ge(dve_link, count("link"))
                    v.tensor_tensor(BK.rearrange("p j c t -> p (j c) t")[:, :, CHUNK:P], flat(Ks), flat(A3), ALU.mult)

                def fold(_):
                    ar, bk = (w.rearrange("p j c t -> p (j c) t") for w in (AR, BK))
                    v.tensor_copy(pend[:, :, :], A2.rearrange("p j (c t) -> p j c t", t=CHUNK)[:, :, :, CHUNK - 1])
                    v.scalar_tensor_tensor(ar[:, :, 0:CHUNK], flat(KK), -1.0, flat(A1), ALU.mult, ALU.mult)
                    v.scalar_tensor_tensor(TMP, TA, 1.0, KK, ALU.add, ALU.mult).then_inc(dve_link, 1)
                    dve.wait_ge(dve_link, count("link"))
                    v.scalar_tensor_tensor(bk[:, :, 0:CHUNK], flat(TMP), 0.5, flat(A3), ALU.mult, ALU.mult) \
                        .then_inc(dve_done["fold"], 1)
                    dve.wait_ge(dve_done["fold"], count("fold"))

                def r_in(_):
                    dve.wait_ge(*taken("r"))
                    lerp(Rs, 0)
                    v.tensor_tensor(AR.rearrange("p j c t -> p (j c) t")[:, :, CHUNK:P], flat(Rs), flat(A2), ALU.mult)
                    for j in range(PAIRS):
                        last = v.scalar_tensor_tensor(TMP[:, j, :], Rs[:, j, :], pc("r_k", j), Ks[:, j, :], ALU.mult,
                                                      ALU.mult)
                    last.then_inc(dve_done["bonus_in"], 1)
                    dve.wait_ge(dve_done["bonus_in"], count("bonus_in"))

                def bonus(_):
                    dve.wait_ge(pe_done["bonus"], 1)
                    dve.wait_ge(pool_done["v_done"], 1)
                    v.tensor_tensor(BON, pair_tiles(4), V, ALU.mult).then_inc(dve_done["bonus"], 1)
                    dve.wait_ge(dve_done["bonus"], count("bonus"))

                def merge(T, b, signal, n):
                    dve.wait_ge(pe_done[signal], n + 1)
                    for p in range(2):
                        d = T[:, p::2, :, :].rearrange("p j c t -> p j (c t)")
                        last = v.tensor_tensor(d, d, bank(b + p).rearrange("p (j t) -> p j t", j=PAIRS), ALU.add)
                    last.then_inc(dve_done[signal], 1)
                    dve.wait_ge(dve_done[signal], count(signal))

                def merge_u(n):
                    merge(Tu, 6, "merge_u", n)

                def merge_l(n):
                    merge(Tl, 4, "merge_l", n)

                def chunk_m(c):
                    dve.wait_ge(pe_done["chunk_m"], c + 1)
                    for p in range(2):
                        last = v.tensor_tensor(MC[:, c % 2, p::2, :], bank(4 + p).rearrange("p (j t) -> p j t", j=PAIRS),
                                               cmask.unsqueeze(1).broadcast_to([P, PAIRS, P]), ALU.mult)
                    last.then_inc(dve_done["chunk_m"], 1)
                    dve.wait_ge(dve_done["chunk_m"], count("chunk_m"))

                def chunk_z(c):
                    dve.wait_ge(pe_done["chunk_z"], c + 1)
                    zs = []
                    for p in range(2):
                        rows = slice(64 * p, 64 * p + 64)
                        z = Z[rows, :, 64 * p:64 * p + 64]
                        zs.append((z, rows))
                        last = v.tensor_tensor(z, z, psum[rows, 5, 0:PAIRS * HD].rearrange("p (j t) -> p j t", j=PAIRS),
                                               ALU.add)
                    last.then_inc(dve_link, 1)
                    dve.wait_ge(dve_link, count("link"))
                    for z, rows in zs:
                        last = v.tensor_tensor(z, z, pend[rows, :, c:c + 1].broadcast_to([64, PAIRS, HD]), ALU.mult)
                    last.then_inc(dve_done["chunk_z"], 1)
                    dve.wait_ge(dve_done["chunk_z"], count("chunk_z"))

                def gn_mean(_):
                    dve.wait_ge(pe_done["gn_mean"], 1)
                    v.scalar_tensor_tensor(OT.rearrange("p j s -> p (j s)").rearrange("p (b c) -> p b c", b=2),
                                           psum[:, 4:6, :], -1.0 / HD,
                                           OT.rearrange("p j s -> p (j s)").rearrange("p (b c) -> p b c", b=2),
                                           ALU.mult, ALU.add).then_inc(dve_done["gn_mean"], 1)
                    dve.wait_ge(dve_done["gn_mean"], count("gn_mean"))

                def gn_var(_):
                    dve.wait_ge(pe_done["gn_var"], 1)
                    v.tensor_scalar(S8b, psum[:, 4, 0:TT * HEADS], 1.0 / HD, LNX_EPS, ALU.mult, ALU.add) \
                        .then_inc(dve_done["gn_var"], 1)
                    dve.wait_ge(dve_done["gn_var"], count("gn_var"))

                def gn_T(_):
                    dve.wait_ge(pe_done["gn_T"], 1)
                    v.tensor_copy(R8bT, psum[0:HEADS, 4, 0:SEQ]).then_inc(dve_done["gn_T"], 1)
                    dve.wait_ge(dve_done["gn_T"], count("gn_T"))

                def gn_scale(_):
                    dve.wait_ge(pe_done["gn_scale"], 1)
                    v.tensor_tensor(OT, OT, pair_tiles(4), ALU.mult).then_inc(dve_done["gn_scale"], 1)
                    dve.wait_ge(dve_done["gn_scale"], count("gn_scale"))
                    per_pair(OT, OT, lambda j: pc("lnx_w", j), lambda j: pc("lnx_b", j)).then_inc(dve_link, 1)
                    dve.wait_ge(dve_link, count("link"))
                    v.tensor_tensor(OT, OT, BON, ALU.add).then_inc(dve_link, 1)
                    dve.wait_ge(dve_link, count("link"))
                    v.tensor_tensor(OSQ, OT, G, ALU.mult).then_inc(dve_done["rw_o"], 1)
                    dve.wait_ge(dve_done["rw_o"], count("rw_o"))

                def scores(b, pair):
                    dve.wait_ge(pe_done["scores"], 4 * (b - 1) + pair + 1)
                    s0 = 20 * ((4 * (b - 1) + pair) % 2)
                    mx = soft[:, s0 + 12:s0 + 16].rearrange("p (h m) -> p h m", m=TT)
                    v.tensor_tensor(probs, psum[:, 6:8, 0:384], amask[b].unsqueeze(1).broadcast_to([P, 2, 384]),
                                    ALU.add).then_inc(dve_link, 1)
                    dve.wait_ge(dve_link, count("link"))
                    v.reduce_max(mx[:, :, 0], probs[:, :, 0:P], AX.X)
                    v.reduce_max(mx[:, :, 1], probs[:, :, P:3 * P], AX.X).then_inc(dve_link, 1)
                    dve.wait_ge(dve_link, count("link"))
                    nb = soft[:, s0:s0 + 4]
                    if b == 1:
                        last = v.tensor_scalar(nb, soft[:, s0 + 12:s0 + 16], -HD ** -0.5, None, ALU.mult)
                    else:
                        sink = sinks[:, 2 * pair:2 * pair + 2].unsqueeze(2).broadcast_to([P, 2, TT])
                        v.tensor_scalar(mx, mx, HD ** -0.5, None, ALU.mult).then_inc(dve_link, 1)
                        dve.wait_ge(dve_link, count("link"))
                        v.tensor_tensor(mx, mx, sink, ALU.max).then_inc(dve_link, 1)
                        dve.wait_ge(dve_link, count("link"))
                        v.tensor_scalar(nb, soft[:, s0 + 12:s0 + 16], -1.0, None, ALU.mult)
                        last = v.tensor_tensor(soft[:, s0 + 16:s0 + 20].rearrange("p (h m) -> p h m", m=TT), sink, mx,
                                               ALU.subtract)
                    last.then_inc(dve_done["scores"], 1)
                    dve.wait_ge(dve_done["scores"], count("scores"))

                def pT(b, pair):
                    dve.wait_ge(pe_done["pT"], 4 * (b - 1) + pair + 1)
                    v.tensor_copy(probsT, psum[:, 6:8, 0:384]).then_inc(dve_done["pT"], 1)
                    dve.wait_ge(dve_done["pT"], count("pT"))

                def pv(b, pair):
                    dve.wait_ge(pe_done["pv"], 4 * (b - 1) + pair + 1)
                    s0 = 20 * ((4 * (b - 1) + pair) % 2)
                    sums, rinv = soft[:, s0 + 4:s0 + 8], soft[:, s0 + 8:s0 + 12]
                    if b == 2:
                        v.tensor_tensor(sums, sums, soft[:, s0 + 16:s0 + 20], ALU.add).then_inc(dve_link, 1)
                        dve.wait_ge(dve_link, count("link"))
                    v.reciprocal(rinv, sums).then_inc(dve_link, 1)
                    dve.wait_ge(dve_link, count("link"))
                    v.tensor_tensor(QTOK[:, :, pair * P:(pair + 1) * P].rearrange("p m (h d) -> p m h d", d=HD),
                                    psum[:, 6, 0:256].rearrange("p (m h d) -> p m h d", m=TT, d=HD),
                                    rinv.rearrange("p (h m) -> p m h", m=TT).unsqueeze(3).broadcast_to([P, TT, 2, HD]),
                                    ALU.mult).then_inc(dve_done["pv"], 1)
                    dve.wait_ge(dve_done["pv"], count("pv"))

                def xmax(h):
                    dve.wait_ge(pe_done["xscores"], h + 1)
                    s0 = 20 * (h % 2)
                    v.reduce_max(soft[:, s0 + 12:s0 + 14], psum[:, 4 + h % 2, :].rearrange("p (m k) -> p m k", m=TT),
                                 AX.X).then_inc(dve_link, 1)
                    dve.wait_ge(dve_link, count("link"))
                    dve.wait_ge(pool_done["rstd"], 2)
                    v.scalar_tensor_tensor(soft[:, s0:s0 + 2], soft[:, s0 + 12:s0 + 14], -1.0, stat[:, 6:8], ALU.mult,
                                           ALU.mult) \
                        .then_inc(dve_done["xmax"], 1)
                    dve.wait_ge(dve_done["xmax"], count("xmax"))

                def xpT(h):
                    dve.wait_ge(pe_done["xpT"], h + 1)
                    v.tensor_copy(XPT[:, h % 2, :, :].rearrange("p k s -> p (k s)"), bank(6 + h % 2)) \
                        .then_inc(dve_done["xpT"], 1)
                    dve.wait_ge(dve_done["xpT"], count("xpT"))

                def xpv(h):
                    dve.wait_ge(pe_done["xpv"], h + 1)
                    s0 = 20 * (h % 2)
                    v.reciprocal(soft[:, s0 + 8:s0 + 10], soft[:, s0 + 4:s0 + 6]).then_inc(dve_link, 1)
                    dve.wait_ge(dve_link, count("link"))
                    v.tensor_tensor(XO[:, :, h * XD:(h + 1) * XD],
                                    psum[:, 4 + h % 2, 0:TT * XD].rearrange("p (m d) -> p m d", m=TT),
                                    soft[:, s0 + 8:s0 + 10].unsqueeze(2).broadcast_to([P, TT, XD]), ALU.mult) \
                        .then_inc(dve_done["xpv"], 1)
                    dve.wait_ge(dve_done["xpv"], count("xpv"))

                parts = {"params": params, "pre_scale": pre_scale, "pre_T": pre_T, "split_low": split_low,
                         "oT": oT_, "yT": yT, "xoT": xoT, "hiddenT": hiddenT, "mem_scale": mem_scale, "mem_T": mem_T, "v_down": v_down_split,
                         "rw_low": rw_low,
                         "lora_tanh": lora_lerp, "vres_down": vres_lerp, "lora_sig": lora_sig, "decay": scan,
                         "k_in": k_in, "v_in": v_in, "r_in": r_in, "kk_sum": kk_sum, "kk_T": kk_T, "kk_scale": kk_scale,
                         "fold_k": fold_k, "fold": fold, "bonus": bonus, "merge_u": merge_u, "merge_l": merge_l, "chunk_m": chunk_m,
                         "chunk_z": chunk_z, "gn_mean": gn_mean, "gn_var": gn_var, "gn_T": gn_T, "gn_scale": gn_scale,
                         "scores": scores, "pT": pT, "pv": pv, "xscores": xmax, "xpT": xpT, "xpv": xpv}
                for kind, *which in ORDER:
                    if kind == "gemm":
                        name, q = which
                        if q == pieces(name) - 1:
                            if name in POST_HALVES:
                                for h in POST_HALVES[name]:
                                    times_gain(name, h)
                                if name in POST_AFTER:
                                    post(POST_AFTER.index(name) + 1)
                            elif TAKER[name] == "dve":
                                take(name)
                    elif kind in parts:
                        parts[kind](*which)
                v.memset(not_first[:, :], 0.5)
                dve.drain().then_inc(layer_end, 1)
                dve.wait_ge(layer_end, l * 4 + 4)
                dve.sem_inc(wait_carrier, 1)
                dve.sem_clear(range(nums[0], nums[-1] + 1))
                dve.drain().then_inc(layer_clear, 1)

        @block.gpsimd
        def _(pool):
            g = nc.gpsimd
            g.memset(neg_half[:, :], -0.5)
            g.memset(v_first[:, :, :], 0.0).then_inc(pool_start, 1)

            def rstd(src, dst, n, link, value):
                g.tensor_scalar(dst, src, 1.0 / D, NORM_EPS, ALU.mult, ALU.add).then_inc(link, 1)
                pool.wait_ge(link, value)
                return g.tensor_tensor(dst, dst, neg_half[:, 0:n], ALU.pow)

            pool.wait_ge(pool_start, 1)

            with pool.Fori(0, DEPTH) as l:
                count = Counts()

                def load_gain(which):
                    pool.dma_start(post_gain[:, :], t[which][l].partition_broadcast(P)).then_inc(post_gain_in, 16)

                g.memset(U[:, :, 0:1], 0.0)
                g.memset(U2[:, :, 0:1], 0.0)
                g.memset(UV[:, 0:1], 0.0)
                g.memset(VT[:, :, 0:CHUNK], 0.0)
                g.memset(RESET, 1.0).then_inc(pool_link, 1)
                pool.wait_ge(pool_link, count("link"))
                g.memset(RESET.rearrange("p (c t) -> p c t", t=CHUNK)[:, :, 0:1], 0.0) \
                    .then_inc(pool_done["zero"], 1)
                pool.wait_ge(pool_done["zero"], count("zero"))
                def pre_scale(n):
                    pool.wait_ge(act_done["squares"], n + 1)
                    last = rstd(stat[:, 0:2], stat[:, 4:6], TT, pool_link, count("link"))
                    if n == 1:
                        last.then_inc(pool_link, 1)
                        pool.wait_ge(pool_link, count("link"))
                        last = g.tensor_scalar(stat[:, 6:8], stat[:, 4:6], XD ** -0.5, None, ALU.mult)
                    last.then_inc(pool_done["rstd"], 1)
                    pool.wait_ge(pool_done["rstd"], count("rstd"))

                def post_rstd(n):
                    pool.wait_ge(act_done["post_squares"], 4 * n)
                    s = stat[:, 8:12].rearrange("p (m h) -> p m h", h=2)
                    g.tensor_tensor(stat[:, 16:18], s[:, :, 0], s[:, :, 1], ALU.add).then_inc(pool_link, 1)
                    pool.wait_ge(pool_link, count("link"))
                    rstd(stat[:, 16:18], stat[:, 20:22], TT, pool_link, count("link")).then_inc(pool_done["post_rstd"], 1)
                    pool.wait_ge(pool_done["post_rstd"], count("post_rstd"))
                    if n < 3:
                        pool.wait_ge(dve_done["post"], n)
                        load_gain(("norm_xattn_post", "norm_mlp_post")[n - 1])

                def v_gate(_):
                    pool.wait_ge(act_done["vres_up"], 1)
                    pool.wait_ge(dve_done["lerp"], 2)
                    g.tensor_scalar(VG, VG, 1.0, not_first[:, 0:1], ALU.add, ALU.mult)
                    g.tensor_tensor(VD, v_first[:, :, :], V, ALU.subtract).then_inc(pool_link, 1)
                    pool.wait_ge(pool_link, count("link"))
                    g.tensor_tensor(VD, VD, VG, ALU.mult).then_inc(pool_link, 1)
                    pool.wait_ge(pool_link, count("link"))
                    g.tensor_tensor(V, V, VD, ALU.add).then_inc(pool_done["v_done"], 1)
                    pool.wait_ge(pool_done["v_done"], count("v_done"))
                    g.tensor_copy(v_first[:, :, :], V).then_inc(pool_link, 1)
                    pool.wait_ge(pool_link, count("link"))

                def mem_rstd(_):
                    pool.wait_ge(act_done["mem_squares"], 1)
                    rstd(stat[:, 12:14], stat[:, 14:16], TT, pool_link, count("link")).then_inc(pool_done["mem_rstd"], 1)
                    pool.wait_ge(pool_done["mem_rstd"], count("mem_rstd"))

                def kk_sq(_):
                    pool.wait_ge(dve_done["kk"], 1)
                    g.tensor_tensor(TMP, KK, KK, ALU.mult).then_inc(pool_done["kk_sq"], 1)
                    pool.wait_ge(pool_done["kk_sq"], count("kk_sq"))

                def kk_pow(_):
                    pool.wait_ge(dve_done["kk_sum"], 1)
                    g.tensor_tensor(R8, S8, neg_half[:, 0:TT * HEADS], ALU.pow) \
                        .then_inc(pool_done["kk_pow"], 1)
                    pool.wait_ge(pool_done["kk_pow"], count("kk_pow"))

                def zero(_):
                    pool.wait_ge(pe_done["bonus"], 1)
                    pool.wait_ge(dve_done["bonus_in"], 1)
                    g.memset(SV[0:64, :, :, :], 0.0)
                    g.memset(Z, 0.0)
                    for T in (Tu, Tl):
                        last = g.tensor_copy(T.rearrange("p h c t -> p (h c) t"),
                                             ident2.unsqueeze(1).broadcast_to([P, 2 * HEADS, CHUNK]))
                    last.then_inc(pool_done["zero"], 1)
                    pool.wait_ge(pool_done["zero"], count("zero"))

                def mask(n):
                    if n == 0:
                        pool.wait_ge(act_done["low"], 1)
                    else:
                        pool.wait_ge(pe_done["merge_p"], n)
                    g.tensor_tensor(El.rearrange("p h c t -> p (h c) t"), Nl.rearrange("p h c t -> p (h c) t"),
                                    level[:, n, :].unsqueeze(1).broadcast_to([P, 2 * HEADS, CHUNK]), ALU.mult) \
                        .then_inc(pool_done["mask"], 1)
                    pool.wait_ge(pool_done["mask"], count("mask"))

                def gn_sq(_):
                    pool.wait_ge(dve_done["gn_mean"], 1)
                    g.tensor_tensor(OSQ, OT, OT, ALU.mult).then_inc(pool_done["gn_sq"], 1)
                    pool.wait_ge(pool_done["gn_sq"], count("gn_sq"))

                def gn_pow(_):
                    pool.wait_ge(dve_done["gn_var"], 1)
                    g.tensor_tensor(R8b, S8b, neg_half[:, 0:TT * HEADS], ALU.pow).then_inc(pool_done["gn_pow"], 1)
                    pool.wait_ge(pool_done["gn_pow"], count("gn_pow"))

                parts = {"pre_scale": pre_scale, "k_in": kk_sq, "kk_sum": kk_pow, "v_gate": v_gate, "zero": zero, "merge_p": mask,
                         "gn_mean": gn_sq, "gn_var": gn_pow, "mem_scale": mem_rstd}
                for kind, *which in ORDER:
                    if kind == "gemm":
                        name, q = which
                        if q == pieces(name) - 1 and name == "branch01":
                            pool.wait_ge(*taken("branch01"))
                            load_gain("norm_mix_post")
                        if q == pieces(name) - 1 and name in POST_AFTER:
                            post_rstd(POST_AFTER.index(name) + 1)
                    elif kind in parts:
                        parts[kind](*which)
                pool.drain().then_inc(layer_end, 1)
                pool.wait_ge(layer_clear, l + 1)


_INS = ["x", "mem", "positions", "norm_mix_pre", "norm_mix_post", "norm_xattn_pre", "norm_xattn_post", "norm_mem",
        "norm_mlp_pre", "norm_mlp_post", "w_in", "rw_mu", "rw_w0", "rw_w_up", "rw_a0", "rw_a_up", "rw_g_up",
        "rw_k_k", "rw_k_a", "rw_r_k", "rw_lnx_w", "rw_lnx_b", "rw_vres_down", "rw_vres_mu", "rw_v0",
        "rw_vres_up", "sw_sinks", "w_branch", "w_out", "w_xq", "w_xk", "w_xv", "w_xo", "w_up", "w_down"]


def kernel(**inputs):
    import concourse.bacc as _bacc
    from concourse.bass_utils import run_bass_kernel_spmd as _run

    nc = _bacc.Bacc("TRN2", target_bir_lowering=False, num_devices=1)
    arrays, args = {}, {}
    for name, a in [(n, inputs[n]) for n in _INS] + [("consts", constants())]:
        a = np.ascontiguousarray(a)
        arrays[f"in_{name}"] = a
        args[name] = nc.dram_tensor(f"in_{name}", a.shape, mybir.dt.from_np(a.dtype), kind="ExternalInput").ap()
    out = nc.dram_tensor("out_x", (1, SEQ, D), F32, kind="ExternalOutput").ap()
    build(nc, args, out)
    r = _run(nc, [arrays], core_ids=[0])
    return r.results[0]["out_x"]
```
